# Optimizing a Trainium2 kernel written in Bass

```python
import math
import jax, jax.numpy as jnp
from jax import lax
import numpy as np

D_MODEL = 1024
BATCH = 1
SEQ = 256
DEPTH = 1

MEM_LEN = 256
HEAD_DIM = 64
N_HEADS = D_MODEL // HEAD_DIM
N_KV_GROUPS = 4
HEADS_PER_GROUP = N_HEADS // N_KV_GROUPS
CMP_BLOCK = 32
CMP_STRIDE = 16
SEL_BLOCK = 64
SEL_TOP_N = 16
WINDOW = 512
Q_BLOCK = 128
SEL_Q_CHUNK = 16
CONV_CH = D_MODEL
CONV_WIDTH = 31
X_HEADS = 4
X_HEAD_DIM = D_MODEL // X_HEADS
D_FF = int(math.ceil(8 * D_MODEL / 3 / 256)) * 256
REL_BUCKETS = 32
REL_MAX_DIST = 128
EPS = 1e-6

SPLIT_SIZES = (
    2 * CONV_CH,
    N_HEADS * HEAD_DIM,
    N_KV_GROUPS * HEAD_DIM,
    N_KV_GROUPS * HEAD_DIM,
    N_KV_GROUPS * HEAD_DIM,
    N_KV_GROUPS * HEAD_DIM,
    N_KV_GROUPS * HEAD_DIM,
    N_KV_GROUPS * HEAD_DIM,
    3 * N_HEADS,
    D_MODEL,
    D_MODEL,
)
N_IN = sum(SPLIT_SIZES)
SPLIT_POINTS = tuple(int(v) for v in np.cumsum(SPLIT_SIZES)[:-1])


def rms_norm(x, g):
    xf = x.astype(jnp.float32)
    y = xf * lax.rsqrt(jnp.mean(xf * xf, axis=-1, keepdims=True) + EPS)
    return (y * g.astype(jnp.float32)).astype(x.dtype)

def layer_norm(x, g, b):
    xf = x.astype(jnp.float32)
    mu = jnp.mean(xf, axis=-1, keepdims=True)
    xc = xf - mu
    y = xc * lax.rsqrt(jnp.mean(xc * xc, axis=-1, keepdims=True) + EPS)
    return (y * g.astype(jnp.float32) + b.astype(jnp.float32)).astype(x.dtype)

def t5_bucket(dist):
    n = jnp.maximum(dist, 0)
    max_exact = REL_BUCKETS // 2
    nf = jnp.maximum(n, 1).astype(jnp.float32)
    large = max_exact + (jnp.log(nf / max_exact) / math.log(REL_MAX_DIST / max_exact)
                         * (REL_BUCKETS - max_exact)).astype(jnp.int32)
    large = jnp.minimum(large, REL_BUCKETS - 1)
    return jnp.where(n < max_exact, n, large)

def masked_softmax(s, mask):
    s = jnp.where(mask, s, -1e30)
    m = jnp.max(s, axis=-1, keepdims=True)
    p = jnp.where(mask, jnp.exp(s - m), 0.0)
    return p / jnp.maximum(jnp.sum(p, axis=-1, keepdims=True), 1e-30)

def conv_module(u, dw_w, dw_b, ln_g, ln_b, pw_w):
    a, gt = jnp.split(u, 2, axis=-1)
    v = a * jax.nn.sigmoid(gt)
    v = lax.conv_general_dilated(
        v, dw_w[:, None, :], window_strides=(1,),
        padding=((CONV_WIDTH - 1, 0),),
        dimension_numbers=("NWC", "WIO", "NWC"),
        feature_group_count=CONV_CH) + dw_b
    v = jax.nn.silu(layer_norm(v, ln_g, ln_b))
    return v @ pw_w

def compress_blocks(blocks, pos, w1, w2):
    z = blocks + pos[None, None, :, None, :]
    z = jnp.einsum("bnlgd,lde->bnge", z, w1)
    return jax.nn.silu(z) @ w2

def nsa_attention(q, kc, vc, ks, vs, kw, vw, gate_logits, cmp_pos, cmp_w1, cmp_w2, rel_bias):
    B, S = q.shape[0], q.shape[1]
    G, R, Dh = N_KV_GROUPS, HEADS_PER_GROUP, HEAD_DIM
    scale = 1.0 / math.sqrt(Dh)
    qg = q.reshape(B, S, G, R, Dh)
    t = jnp.arange(S)

    n_cmp = (S - CMP_BLOCK) // CMP_STRIDE + 1
    cidx = np.arange(n_cmp)[:, None] * CMP_STRIDE + np.arange(CMP_BLOCK)[None, :]
    k_cmp = compress_blocks(kc[:, cidx], cmp_pos[0], cmp_w1[0], cmp_w2[0])
    v_cmp = compress_blocks(vc[:, cidx], cmp_pos[1], cmp_w1[1], cmp_w2[1])
    c_end = jnp.arange(n_cmp) * CMP_STRIDE + CMP_BLOCK - 1
    dist_c = t[:, None] - c_end[None, :]
    bias_c = rel_bias[t5_bucket(dist_c)].reshape(S, n_cmp, G, R).transpose(2, 3, 0, 1)
    s_c = jnp.einsum("bsgrd,bngd->bgrsn", qg, k_cmp).astype(jnp.float32) * scale + bias_c
    p_cmp = masked_softmax(s_c, dist_c >= 0)
    o_cmp = jnp.einsum("bgrsn,bngd->bsgrd", p_cmp.astype(v_cmp.dtype), v_cmp)

    n_sel = S // SEL_BLOCK
    top_n = min(SEL_TOP_N, n_sel)
    jj = np.arange(n_cmp)[:, None] * CMP_STRIDE
    mm0 = np.arange(n_sel)[None, :] * SEL_BLOCK
    overlap = ((jj < mm0 + SEL_BLOCK) & (jj + CMP_BLOCK > mm0)).astype(np.float32)
    imp = jnp.einsum("bgrsn,nm->bsgm", p_cmp, jnp.asarray(overlap))
    blk_t = (t // SEL_BLOCK)[:, None]
    mm = jnp.arange(n_sel)[None, :]
    forced = (mm == 0) | (mm == blk_t) | (mm == blk_t - 1)
    valid = mm <= blk_t
    score = jnp.where(forced[None, :, None, :], jnp.inf,
                      jnp.where(valid[None, :, None, :], imp, -jnp.inf))
    _, sel_idx = lax.top_k(score, top_n)

    ksg = ks.reshape(B, n_sel, SEL_BLOCK, G, Dh).transpose(0, 3, 1, 2, 4)
    vsg = vs.reshape(B, n_sel, SEL_BLOCK, G, Dh).transpose(0, 3, 1, 2, 4)
    bias_g = rel_bias.reshape(REL_BUCKETS, G, R)
    nc = S // SEL_Q_CHUNK
    q_ch = qg.reshape(B, nc, SEL_Q_CHUNK, G, R, Dh).swapaxes(0, 1)
    i_ch = sel_idx.reshape(B, nc, SEL_Q_CHUNK, G, top_n).swapaxes(0, 1)
    starts = jnp.arange(nc) * SEL_Q_CHUNK
    b_ix = jnp.arange(B)[:, None, None, None]
    g_ix = jnp.arange(G)[None, None, :, None]
    n_keys = top_n * SEL_BLOCK

    def sel_chunk(args):
        qc, ic, st = args
        kg = ksg[b_ix, g_ix, ic].reshape(B, SEL_Q_CHUNK, G, n_keys, Dh)
        vg = vsg[b_ix, g_ix, ic].reshape(B, SEL_Q_CHUNK, G, n_keys, Dh)
        kpos = (ic[..., None] * SEL_BLOCK + jnp.arange(SEL_BLOCK)).reshape(B, SEL_Q_CHUNK, G, n_keys)
        tq = st + jnp.arange(SEL_Q_CHUNK)
        dist = tq[None, :, None, None] - kpos
        bias = bias_g[t5_bucket(dist), g_ix]
        s = jnp.einsum("bqgrd,bqgkd->bqgrk", qc, kg).astype(jnp.float32) * scale \
            + bias.swapaxes(-1, -2)
        p = masked_softmax(s, (dist >= 0)[:, :, :, None, :])
        return jnp.einsum("bqgrk,bqgkd->bqgrd", p.astype(vg.dtype), vg)

    o_slc = lax.map(sel_chunk, (q_ch, i_ch, starts)).swapaxes(0, 1).reshape(B, S, G, R, Dh)

    nq = S // Q_BLOCK
    kwp = jnp.pad(kw, ((0, 0), (WINDOW, 0), (0, 0), (0, 0)))
    vwp = jnp.pad(vw, ((0, 0), (WINDOW, 0), (0, 0), (0, 0)))
    q_bl = qg.reshape(B, nq, Q_BLOCK, G, R, Dh).swapaxes(0, 1)

    def win_block(args):
        qb, i = args
        start = i * Q_BLOCK
        kb = lax.dynamic_slice_in_dim(kwp, start, Q_BLOCK + WINDOW, axis=1)
        vb = lax.dynamic_slice_in_dim(vwp, start, Q_BLOCK + WINDOW, axis=1)
        tq = start + jnp.arange(Q_BLOCK)
        kpos = start - WINDOW + jnp.arange(Q_BLOCK + WINDOW)
        dist = tq[:, None] - kpos[None, :]
        mask = (dist >= 0) & (dist < WINDOW) & (kpos[None, :] >= 0)
        bias = rel_bias[t5_bucket(dist)].reshape(Q_BLOCK, Q_BLOCK + WINDOW, G, R).transpose(2, 3, 0, 1)
        s = jnp.einsum("bqgrd,bkgd->bgrqk", qb, kb).astype(jnp.float32) * scale + bias
        p = masked_softmax(s, mask)
        return jnp.einsum("bgrqk,bkgd->bqgrd", p.astype(vb.dtype), vb)

    o_win = lax.map(win_block, (q_bl, jnp.arange(nq))).swapaxes(0, 1).reshape(B, S, G, R, Dh)

    g = jax.nn.sigmoid(gate_logits).reshape(B, S, 3, G, R, 1)
    o = g[:, :, 0] * o_cmp + g[:, :, 1] * o_slc + g[:, :, 2] * o_win
    return o.reshape(B, S, N_HEADS * HEAD_DIM)

def hybrid_mixer(h, w_in, conv_dw_w, conv_dw_b, conv_ln_g, conv_ln_b, conv_pw_w,
                 cmp_pos, cmp_w1, cmp_w2, w_out, rel_bias):
    B, S = h.shape[0], h.shape[1]
    (u_conv, q, kc, vc, ks, vs, kw, vw, g_nsa_heads, g_conv, g_attn) = jnp.split(
        h @ w_in, SPLIT_POINTS, axis=-1)
    kv_shape = (B, S, N_KV_GROUPS, HEAD_DIM)
    conv_out = conv_module(u_conv, conv_dw_w, conv_dw_b, conv_ln_g, conv_ln_b, conv_pw_w)
    nsa_out = nsa_attention(
        q.reshape(B, S, N_HEADS, HEAD_DIM),
        kc.reshape(kv_shape), vc.reshape(kv_shape), ks.reshape(kv_shape),
        vs.reshape(kv_shape), kw.reshape(kv_shape), vw.reshape(kv_shape),
        g_nsa_heads.reshape(B, S, 3, N_HEADS), cmp_pos, cmp_w1, cmp_w2, rel_bias)
    y = jax.nn.sigmoid(g_conv) * conv_out + jax.nn.sigmoid(g_attn) * nsa_out
    return y @ w_out

def cross_attention(h, mem, wq, wkv, wo):
    B, S = h.shape[0], h.shape[1]
    M = mem.shape[1]
    q = (h @ wq).reshape(B, S, X_HEADS, X_HEAD_DIM)
    k, v = jnp.split(mem @ wkv, 2, axis=-1)
    k = k.reshape(B, M, X_HEADS, X_HEAD_DIM)
    v = v.reshape(B, M, X_HEADS, X_HEAD_DIM)
    s = jnp.einsum("bshd,bmhd->bhsm", q, k).astype(jnp.float32) / math.sqrt(X_HEAD_DIM)
    p = jax.nn.softmax(s, axis=-1).astype(v.dtype)
    o = jnp.einsum("bhsm,bmhd->bshd", p, v).reshape(B, S, X_HEADS * X_HEAD_DIM)
    return o @ wo

def swiglu(h, w_in, w_out):
    a, b = jnp.split(h @ w_in, 2, axis=-1)
    return (jax.nn.silu(a) * b) @ w_out

def first_inputs(seed: int = 0) -> dict:
    key = jax.random.key(seed)
    ks = jax.random.split(key, 24)
    f32 = jnp.float32

    def nrm(k, shape, scale):
        return jax.random.normal(k, shape, f32) * scale

    def gain(k, shape):
        return 1.0 + 0.02 * jax.random.normal(k, shape, f32)

    return {
        "x": jax.random.normal(ks[0], (BATCH, SEQ, D_MODEL), f32),
        "mem": jax.random.normal(ks[1], (BATCH, MEM_LEN, D_MODEL), f32),
        "norm_mix_g": gain(ks[2], (DEPTH, D_MODEL)),
        "w_in": nrm(ks[3], (DEPTH, D_MODEL, N_IN), D_MODEL ** -0.5),
        "conv_dw_w": nrm(ks[4], (DEPTH, CONV_WIDTH, CONV_CH), CONV_WIDTH ** -0.5),
        "conv_dw_b": nrm(ks[5], (DEPTH, CONV_CH), 0.02),
        "conv_ln_g": gain(ks[6], (DEPTH, CONV_CH)),
        "conv_ln_b": nrm(ks[7], (DEPTH, CONV_CH), 0.02),
        "conv_pw_w": nrm(ks[8], (DEPTH, CONV_CH, D_MODEL), CONV_CH ** -0.5),
        "cmp_pos": nrm(ks[9], (DEPTH, 2, CMP_BLOCK, HEAD_DIM), 0.1),
        "cmp_w1": nrm(ks[10], (DEPTH, 2, CMP_BLOCK, HEAD_DIM, HEAD_DIM), (CMP_BLOCK * HEAD_DIM) ** -0.5),
        "cmp_w2": nrm(ks[11], (DEPTH, 2, HEAD_DIM, HEAD_DIM), HEAD_DIM ** -0.5),
        "w_out": nrm(ks[12], (DEPTH, D_MODEL, D_MODEL), D_MODEL ** -0.5),
        "norm_x_g": gain(ks[13], (DEPTH, D_MODEL)),
        "xq_w": nrm(ks[14], (DEPTH, D_MODEL, X_HEADS * X_HEAD_DIM), D_MODEL ** -0.5),
        "xkv_w": nrm(ks[15], (DEPTH, D_MODEL, 2 * X_HEADS * X_HEAD_DIM), D_MODEL ** -0.5),
        "xo_w": nrm(ks[16], (DEPTH, X_HEADS * X_HEAD_DIM, D_MODEL), (X_HEADS * X_HEAD_DIM) ** -0.5),
        "norm_ffn_g": gain(ks[17], (DEPTH, D_MODEL)),
        "ffn_in_w": nrm(ks[18], (DEPTH, D_MODEL, 2 * D_FF), D_MODEL ** -0.5),
        "ffn_out_w": nrm(ks[19], (DEPTH, D_FF, D_MODEL), D_FF ** -0.5),
        "rel_bias": nrm(ks[20], (REL_BUCKETS, N_HEADS), 0.5),
        "final_norm_g": gain(ks[21], (D_MODEL,)),
    }

def first_block(x, mem, norm_mix_g, w_in, conv_dw_w, conv_dw_b, conv_ln_g, conv_ln_b,
              conv_pw_w, cmp_pos, cmp_w1, cmp_w2, w_out, norm_x_g, xq_w, xkv_w, xo_w,
              norm_ffn_g, ffn_in_w, ffn_out_w, rel_bias, final_norm_g):
    for l in range(DEPTH):
        h = rms_norm(x, norm_mix_g[l])
        x = x + hybrid_mixer(h, w_in[l], conv_dw_w[l], conv_dw_b[l], conv_ln_g[l], conv_ln_b[l],
                             conv_pw_w[l], cmp_pos[l], cmp_w1[l], cmp_w2[l], w_out[l], rel_bias)
        h = rms_norm(x, norm_x_g[l])
        x = x + cross_attention(h, mem, xq_w[l], xkv_w[l], xo_w[l])
        h = rms_norm(x, norm_ffn_g[l])
        x = x + swiglu(h, ffn_in_w[l], ffn_out_w[l])
    return rms_norm(x, final_norm_g)


D_MIX = D_MODEL
D_A = D_MIX // 2
D_B = D_MIX - D_A
A_GROUPS = 8
A_GROUP_DIM = D_A // A_GROUPS
CHUNK = 128
B_HEADS = 8
HEAD_DIM_2 = D_B // B_HEADS
DILATED_BRANCHES = ((128, 1), (512, 4), (2048, 16))
ROPE_THETA = 10000.0
D_IN = 2 * D_A + 3 * D_B
N_KEYS = 128
N_EXPERTS = N_KEYS * N_KEYS
PEER_HEADS = 8
PEER_TOPK = 16
D_KEY = 256
PEER_TOKEN_BLOCK = 128


def rms_norm_2(x, g):
    xf = x.astype(jnp.float32)
    y = xf * lax.rsqrt(jnp.mean(xf * xf, axis=-1, keepdims=True) + EPS)
    return (y * g.astype(jnp.float32)).astype(x.dtype)

def layer_norm_2(x, g, b):
    xf = x.astype(jnp.float32)
    mu = jnp.mean(xf, axis=-1, keepdims=True)
    var = jnp.mean(jnp.square(xf - mu), axis=-1, keepdims=True)
    y = (xf - mu) * lax.rsqrt(var + EPS)
    return (y * g.astype(jnp.float32) + b.astype(jnp.float32)).astype(x.dtype)

def rope_tables(seq):
    pos = jnp.arange(seq, dtype=jnp.float32)
    inv = 1.0 / (ROPE_THETA ** (jnp.arange(0, HEAD_DIM_2, 2, dtype=jnp.float32) / HEAD_DIM_2))
    ang = pos[:, None] * inv[None, :]
    return jnp.cos(ang)[:, None, :], jnp.sin(ang)[:, None, :]

def apply_rope(t, cos, sin):
    tf = t.astype(jnp.float32)
    t1, t2 = tf[..., :HEAD_DIM_2 // 2], tf[..., HEAD_DIM_2 // 2:]
    return jnp.concatenate([t1 * cos - t2 * sin, t2 * cos + t1 * sin], axis=-1).astype(t.dtype)

def spatial_gating(u, v, ln_g, ln_b, w_s, b_s):
    B, S, _ = u.shape
    v = layer_norm_2(v, ln_g, ln_b)
    vc = v.reshape(B, S // CHUNK, CHUNK, A_GROUPS, A_GROUP_DIM)
    mixed = jnp.einsum('gpq,bnqgc->bnpgc', w_s, vc) + b_s.T[None, None, :, :, None]
    return u * mixed.reshape(B, S, D_A)

def to_residue(t, d):
    B, S = t.shape[:2]
    t = t.reshape((B, S // d, d) + t.shape[2:])
    t = jnp.swapaxes(t, 1, 2)
    return t.reshape((B * d, S // d) + t.shape[3:])

def from_residue(t, d, B):
    L = t.shape[1]
    t = t.reshape((B, d, L) + t.shape[2:])
    t = jnp.swapaxes(t, 1, 2)
    return t.reshape((B, L * d) + t.shape[3:])

def banded_attention(q, k, v, half_window):
    N, L, H, hd = q.shape
    blk = half_window
    nb = -(-L // blk)
    pad = nb * blk - L
    qb = jnp.pad(q, ((0, 0), (0, pad), (0, 0), (0, 0))).reshape(N, nb, blk, H, hd)
    kp = jnp.pad(k, ((0, 0), (blk, pad + blk), (0, 0), (0, 0))).reshape(N, nb + 2, blk, H, hd)
    vp = jnp.pad(v, ((0, 0), (blk, pad + blk), (0, 0), (0, 0))).reshape(N, nb + 2, blk, H, hd)
    kw = jnp.concatenate([kp[:, :-2], kp[:, 1:-1], kp[:, 2:]], axis=2)
    vw = jnp.concatenate([vp[:, :-2], vp[:, 1:-1], vp[:, 2:]], axis=2)
    s = jnp.einsum('nbqhd,nbkhd->nbhqk', qb, kw).astype(jnp.float32) * (HEAD_DIM_2 ** -0.5)
    blocks = jnp.arange(nb)[:, None] * blk
    qpos = blocks + jnp.arange(blk)[None, :]
    kpos = blocks - blk + jnp.arange(3 * blk)[None, :]
    rel = kpos[:, None, :] - qpos[:, :, None]
    valid = (jnp.abs(rel) <= half_window) & (kpos >= 0)[:, None, :] & (kpos < L)[:, None, :]
    s = jnp.where(valid[None, :, None], s, -jnp.inf)
    m = jnp.max(s, axis=-1, keepdims=True)
    p = jnp.exp(s - m)
    l = jnp.sum(p, axis=-1)
    o = jnp.einsum('nbhqk,nbkhd->nbqhd', p, vw.astype(jnp.float32))
    l_t = jnp.swapaxes(l, 2, 3)
    o = o / l_t[..., None]
    lse = jnp.swapaxes(m[..., 0], 2, 3) + jnp.log(l_t)
    o = o.reshape(N, nb * blk, H, hd)[:, :L]
    lse = lse.reshape(N, nb * blk, H)[:, :L]
    return o, lse

def dilated_attention(q, k, v):
    B = q.shape[0]
    outs, lses = [], []
    for window, dil in DILATED_BRANCHES:
        half_window = window // (2 * dil)
        o, lse = banded_attention(to_residue(q, dil), to_residue(k, dil), to_residue(v, dil), half_window)
        outs.append(from_residue(o, dil, B))
        lses.append(from_residue(lse, dil, B))
    w = jax.nn.softmax(jnp.stack(lses, axis=0), axis=0)
    return jnp.sum(w[..., None] * jnp.stack(outs, axis=0), axis=0)

def peer(xn, w_query, sub_keys, expert_u, expert_v):
    B, S, D = xn.shape
    xt = xn.reshape((B * S) // PEER_TOKEN_BLOCK, PEER_TOKEN_BLOCK, D)

    def block(xb):
        q = (xb @ w_query).reshape(PEER_TOKEN_BLOCK, PEER_HEADS, 2, D_KEY // 2)
        s = jnp.einsum('thpc,pkc->thpk', q, sub_keys).astype(jnp.float32)
        s1, i1 = lax.top_k(s[:, :, 0], PEER_TOPK)
        s2, i2 = lax.top_k(s[:, :, 1], PEER_TOPK)
        cand = (s1[..., :, None] + s2[..., None, :]).reshape(PEER_TOKEN_BLOCK, PEER_HEADS, PEER_TOPK * PEER_TOPK)
        sc, ci = lax.top_k(cand, PEER_TOPK)
        e = (jnp.take_along_axis(i1, ci // PEER_TOPK, axis=-1) * N_KEYS
             + jnp.take_along_axis(i2, ci % PEER_TOPK, axis=-1))
        g = jax.nn.softmax(sc, axis=-1)
        u = expert_u[e]
        act = jax.nn.gelu(jnp.einsum('td,thkd->thk', xb, u).astype(jnp.float32))
        return jnp.einsum('thk,thkd->td', (g * act).astype(xb.dtype), expert_v[e])

    return lax.map(block, xt).reshape(B, S, D)

def second_inputs(seed: int = 0) -> dict:
    key = jax.random.key(seed)
    ks = jax.random.split(key, 17)
    f32 = jnp.float32
    n = lambda k, shape: jax.random.normal(k, shape, dtype=f32)
    return {
        "x": n(ks[0], (BATCH, SEQ, D_MODEL)),
        "norm1_g": 1.0 + 0.02 * n(ks[1], (DEPTH, D_MODEL)),
        "w_in": n(ks[2], (DEPTH, D_MODEL, D_IN)) * D_MODEL ** -0.5,
        "ln_v_g": 1.0 + 0.02 * n(ks[3], (DEPTH, D_A)),
        "ln_v_b": 0.02 * n(ks[4], (DEPTH, D_A)),
        "w_spatial": n(ks[5], (DEPTH, A_GROUPS, CHUNK, CHUNK)) * CHUNK ** -0.5,
        "b_spatial": 0.02 * n(ks[6], (DEPTH, A_GROUPS, CHUNK)),
        "out_norm_a_g": 1.0 + 0.02 * n(ks[7], (DEPTH, D_A)),
        "out_norm_b_g": 1.0 + 0.02 * n(ks[8], (DEPTH, D_B)),
        "w_out": n(ks[9], (DEPTH, D_MIX, D_MODEL)) * D_MIX ** -0.5,
        "norm2_g": 1.0 + 0.02 * n(ks[10], (DEPTH, D_MODEL)),
        "w_query": n(ks[11], (DEPTH, D_MODEL, PEER_HEADS * D_KEY)) * D_MODEL ** -0.5,
        "sub_keys": n(ks[12], (DEPTH, 2, N_KEYS, D_KEY // 2)) * (D_KEY // 2) ** -0.5,
        "expert_u": n(ks[13], (DEPTH, N_EXPERTS, D_MODEL)) * D_MODEL ** -0.5,
        "expert_v": n(ks[14], (DEPTH, N_EXPERTS, D_MODEL)) * PEER_HEADS ** -0.5,
        "final_norm_g": 1.0 + 0.02 * n(ks[15], (D_MODEL,)),
    }

def second_block(x, norm1_g, w_in, ln_v_g, ln_v_b, w_spatial, b_spatial, out_norm_a_g, out_norm_b_g,
              w_out, norm2_g, w_query, sub_keys, expert_u, expert_v, final_norm_g):
    B, S, _ = x.shape
    cos, sin = rope_tables(S)
    for layer in range(DEPTH):
        h = rms_norm_2(x, norm1_g[layer])
        proj = h @ w_in[layer]
        u_a, v_a, q, k, v = jnp.split(
            proj, [D_A, 2 * D_A, 2 * D_A + D_B, 2 * D_A + 2 * D_B], axis=-1)
        a_out = spatial_gating(jax.nn.gelu(u_a), jax.nn.gelu(v_a), ln_v_g[layer], ln_v_b[layer],
                               w_spatial[layer], b_spatial[layer])
        q = apply_rope(q.reshape(B, S, B_HEADS, HEAD_DIM_2), cos, sin)
        k = apply_rope(k.reshape(B, S, B_HEADS, HEAD_DIM_2), cos, sin)
        v = v.reshape(B, S, B_HEADS, HEAD_DIM_2)
        b_out = dilated_attention(q, k, v).reshape(B, S, D_B).astype(x.dtype)
        mix = jnp.concatenate([rms_norm_2(a_out, out_norm_a_g[layer]),
                               rms_norm_2(b_out, out_norm_b_g[layer])], axis=-1)
        x = x + mix @ w_out[layer]
        x = x + peer(rms_norm_2(x, norm2_g[layer]), w_query[layer], sub_keys[layer],
                     expert_u[layer], expert_v[layer])
    return rms_norm_2(x, final_norm_g)


def setup_inputs(seed=0):
    out = dict(first_inputs(seed))
    for name, value in second_inputs(seed + 1).items():
        if name != "x":
            out[name + "_2"] = value
    return out


def reference(
    x, mem, norm_mix_g, w_in, conv_dw_w, conv_dw_b, conv_ln_g, conv_ln_b, conv_pw_w, cmp_pos,
    cmp_w1, cmp_w2, w_out, norm_x_g, xq_w, xkv_w, xo_w, norm_ffn_g, ffn_in_w, ffn_out_w,
    rel_bias, final_norm_g, norm1_g_2, w_in_2, ln_v_g_2, ln_v_b_2, w_spatial_2, b_spatial_2,
    out_norm_a_g_2, out_norm_b_g_2, w_out_2, norm2_g_2, w_query_2, sub_keys_2, expert_u_2,
    expert_v_2, final_norm_g_2,
):
    x = first_block(
        x, mem, norm_mix_g, w_in, conv_dw_w, conv_dw_b, conv_ln_g, conv_ln_b, conv_pw_w,
        cmp_pos, cmp_w1, cmp_w2, w_out, norm_x_g, xq_w, xkv_w, xo_w, norm_ffn_g, ffn_in_w,
        ffn_out_w, rel_bias, final_norm_g,
    )
    return second_block(
        x, norm1_g_2, w_in_2, ln_v_g_2, ln_v_b_2, w_spatial_2, b_spatial_2, out_norm_a_g_2,
        out_norm_b_g_2, w_out_2, norm2_g_2, w_query_2, sub_keys_2, expert_u_2, expert_v_2,
        final_norm_g_2,
    )


_drawn_inputs = setup_inputs


def setup_inputs(seed=0):
    import zlib

    import numpy as np

    out = dict(_drawn_inputs(seed))
    spreads = {}
    factors = {'norm_mix_g': 3.104,
     'conv_ln_g': 2.726,
     'norm_x_g': 6.649,
     'ln_v_g_2': 10.55,
     'ln_v_b_2': 9.861,
     'b_spatial_2': 10.412,
     'out_norm_a_g_2': 10.774,
     'out_norm_b_g_2': 10.305,
     'norm2_g_2': 9.936,
     'final_norm_g_2': 8.178,
     'conv_dw_b': 3.234,
     'conv_ln_b': 4.726,
     'norm_ffn_g': 4.305}
    for name, (base, spread) in spreads.items():
        noise = np.random.default_rng([zlib.crc32(name.encode()), seed]).standard_normal(out[name].shape)
        drawn = base * np.exp(spread * noise) if base else spread * noise
        out[name] = __import__('jax').numpy.asarray(drawn.astype(out[name].dtype))
    for name, factor in factors.items():
        out[name] = (out[name] * factor).astype(out[name].dtype)
    return out
```

```python
from contextlib import ExitStack
import math

import numpy as np
import concourse.bass as bass
from concourse import mybir

F32 = mybir.dt.float32
F32R = mybir.dt.float32r
U32 = mybir.dt.uint32
ALU = mybir.AluOpType
ACT = mybir.ActivationFunctionType
AX = mybir.AxisListType.X

P = 128
S = 256
TT = S // P
D = 1024
KC = D // P
RING = 4
EPS = 1e-6
NEG = -1e30
MAX_FLOOR = -1e29
G, R, HD = 4, 4, 64
NH = G * R
CONV_W = 31
CMP_BLOCK, CMP_STRIDE = 32, 16
NCMP = (S - CMP_BLOCK) // CMP_STRIDE + 1
XH, XHD = 4, 256
FC = 22
H2, HD2 = 8, 64
PH, TOPK, NK = 8, 16, 128
NEXP = 128

STAGES = [("uconv", 16), ("q", 8), ("kc", 2), ("vc", 2), ("ks", 2), ("kw", 2), ("v", 4), ("gates", 1),
          ("gconv", 8), ("gattn", 8), ("xk", 8), ("xv", 8), ("pw", 8), ("wout", 8), ("xq", 8), ("xo", 8),
          ("ffn", 3 * FC), ("ua", 4), ("va", 4), ("q2", 4), ("k2", 4), ("v2", 4), ("wout2", 8),
          ("wq2", 16), ("experts", 2 * NEXP)]
FIRST, UNITS = {}, 0
for _name, _n in STAGES:
    FIRST[_name] = UNITS
    UNITS += _n

(G_MIX, G_X, G_FFN, G_FINAL, G_NORM1, G_NORM2, CONV_B, CONV_LNG, CONV_LNB, G_OUT2) = range(10)


def build(nc, stream, xT_d, memT_d, cols_d, dw_d, onehot_d, relb_d, pos_d, w1_d, w2_d, ident_d, iota_d,
          lnv_d, rope_d, wsT_d, bs_d, lc_d, skT_d, fg_d, out_d):
    ctx = ExitStack()
    with ctx:
        def sb(name, shape, dt=F32):
            return ctx.enter_context(nc.sbuf_tensor(name, shape, dt))

        def sem(name):
            return ctx.enter_context(nc.semaphore(name))

        raw = sb("ring_raw", [P, RING, D])
        w_hi = sb("ring_hi", [P, RING, D], F32R)
        w_lo = sb("ring_lo", [P, RING, D], F32R)
        a_hi = sb("operand_hi", [P, KC, S], F32R)
        a_lo = sb("operand_lo", [P, KC, S], F32R)
        h_hi = sb("hidden_hi", [P, 2, S], F32R)
        h_lo = sb("hidden_lo", [P, 2, S], F32R)
        arena = sb("arena", [P, P * S])
        ident = sb("ident", [P, P])
        ones = sb("ones_mean", [P, P])
        cols = sb("gain_columns", [P, 10, KC])
        std = sb("std", [P, S])
        act2 = sb("act_out", [P, 2, S])
        routeT = sb("routeT", [P, 3, S])
        hot = sb("onehots", [P, 2, 2, 2, P])
        eps = sb("eps", [P, 1])
        mx = sb("row_max", [P, 2, 6])
        sums = sb("row_sum", [P, 2, 6])
        rinv = sb("row_scale", [P, 2, 6])

        def at(offset, *dims):
            n = int(np.prod(dims))
            v = arena[:, offset:offset + n]
            if len(dims) == 2:
                v = v.rearrange("p (a b) -> p a b", a=dims[0])
            elif len(dims) == 3:
                v = v.rearrange("p (a b c) -> p a b c", a=dims[0], b=dims[1])
            elif len(dims) == 4:
                v = v.rearrange("p (a b c d) -> p a b c d", a=dims[0], b=dims[1], c=dims[2])
            return v

        xT = at(0, KC, S)
        hf = at(2048, KC, S)
        sq = at(4096, KC, S)
        cacc = at(6144, KC, S)
        qT = at(8192, KC, S)
        kcT, vcT, ksT, kwT = (at(10240 + 512 * n, 2, S) for n in range(4))
        vrows = at(12288, TT, 512)
        gcon = at(13312, KC, S)
        gatt = at(15360, KC, S)
        bias = at(17408, NH, 384)
        w1 = [at(17408, CMP_BLOCK, P), at(23552, CMP_BLOCK, P)]
        z = [at(21504, CMP_BLOCK, 2, NCMP), at(22464, CMP_BLOCK, 2, NCMP)]
        kx = at(23552, KC, S)
        vx = at(25600, TT, D)
        vconv = at(27648, KC, CONV_W - 1 + S)
        prob = at(29936, 2, 800)
        dw = at(31536, KC, CONV_W)
        w2 = at(31784, 2, P)
        pos = at(32040, 2, CMP_BLOCK)
        cmid = at(32104, 2, 2 * NCMP)
        kcmp = at(32164, 2 * NCMP)
        gates = at(32194, 3, NH, TT)
        vcmp = at(32290, 2, P)
        mean = at(4096, S)
        onehot = at(6144, 512)
        relb = at(6656, NH)
        brow = at(6688, 512)
        pT = at(4096, 2, 768)
        pcT = at(5632, 2, S)
        xprob = at(29936, 2, 512)
        xpT = at(4096, 2, 512)
        ua, va = at(6144, TT, 512), at(7168, TT, 512)
        q2, k2, v2 = (at(8192 + 1024 * n, TT, 512) for n in range(3))
        wsT = at(11264, 8, P)
        lnv = at(12288, 2, 512)
        rope = at(13312, TT, 2, 32)
        bs = at(13440, 8)
        stat = at(13448, 32)
        qk2T = at(13824, 2, 4, S)
        lc = at(15872, TT, S)
        mix = at(16384, 2, TT, 512)
        tmpA = at(18432, TT, 512)
        tmpB = at(19456, TT, 512)
        prob2 = at(20480, 2, 512)
        pT2 = at(21504, 2, 512)
        skT = at(31488, 2, P)
        qq = at(22528, 2 * PH, S)
        sc = at(26624, TT, 2 * PH, NK)
        rest = at(30720, 256)
        cand = at(6144, TT * PH, TOPK, TOPK)
        val = at(10240, TT, PH, 2, TOPK)
        idx = at(10752, TT, PH, 2, TOPK).bitcast(U32)
        idxf = at(11264, TT, PH, 2, TOPK)
        cval = at(11776, TT * PH, TOPK)
        cidx = at(12032, TT * PH, TOPK).bitcast(U32)
        cpart = at(12288, 2, TT * PH * TOPK).bitcast(U32)
        cpartf = at(12800, 2, TT * PH * TOPK)
        pick = at(13824, 3, TT, PH * TOPK)
        eq = at(15872, P, TOPK)
        prod = at(17920, PH, TOPK, TOPK)
        psm = at(19968, TT * PH)
        iota = at(20224, P)
        iota_k = sb("iota_k", [P, P], mybir.dt.bfloat16)
        wall = at(0, P, S)
        fin = at(0, TT, D)
        fsq = at(2048, TT, D)
        fg = at(4096, D)

        bank = [ctx.enter_context(nc.psum_tensor(f"bank{b}", [P, 512], F32)) for b in range(8)]

        bias_d = nc.dram_tensor("bias_rows", [NH, P, 512], F32, kind="Internal")

        landed = [sem(f"unit_landed{s}") for s in range(RING)]
        hi_ready = sem("hi_ready")
        lo_ready = sem("lo_ready")
        unit_done = sem("unit_done")
        bank_free = [sem(f"bank_free{b}") for b in range(8)]
        act_seq, dve_seq, pool_seq = sem("act_seq"), sem("dve_seq"), sem("pool_seq")
        consts_in, const2_in, lnv_in = sem("consts_in"), sem("const2_in"), sem("lnv_in")
        x_in, mem_in = sem("x_in"), sem("mem_in")
        onehot_in = sem("onehot_in")
        w1_in = sem("w1_in")
        init = sem("init")
        norm_sq = sem("norm_sq")
        norm_sum = sem("norm_sum")
        norm_out = sem("norm_out")
        opnd_hi = sem("opnd_hi")
        opnd_ready = sem("opnd_ready")
        brow_done = sem("brow_done")
        brow_sb = sem("brow_sb")
        brow_out = sem("brow_out")
        bias_in = sem("bias_in")
        z_ready = sem("z_ready")
        cmp_h = sem("cmp_h")
        cmp_o = sem("cmp_o")
        taps = sem("taps")
        scores = sem("scores")
        biased = sem("biased")
        exped = sem("exped")
        scale_ready = sem("scale_ready")
        scaled = sem("scaled")
        probsT = sem("probsT")
        attended = sem("attended")
        conv_sum = sem("conv_sum")
        conv_cent = sem("conv_cent")
        conv_var = sem("conv_var")
        conv_ln = sem("conv_ln")
        conv_act = sem("conv_act")
        y_ready = sem("y_ready")
        xs = sem("xs")
        xs_max = sem("xs_max")
        xs_rinv = sem("xs_rinv")
        xs_scaled = sem("xs_scaled")
        xpt = sem("xpt")
        xo_done = sem("xo_done")
        hid_hi = sem("hid_hi")
        hid_ready = sem("hid_ready")
        stat_ready = sem("stat_ready")
        stat_std = sem("stat_std")
        ln2 = sem("ln2")
        mixed = sem("mixed")
        roped = sem("roped")
        qk_t = sem("qk_t")
        s2 = sem("s2")
        s2_biased = sem("s2_biased")
        s2_exp = sem("s2_exp")
        p2t = sem("p2t")
        o2 = sem("o2")
        mix_ready = sem("mix_ready")
        mix_t = sem("mix_t")
        sk_s = sem("sk_s")
        routed = sem("routed")
        route_t = sem("route_t")
        c_exp = sem("c_exp")
        c_sub = sem("c_sub")
        hot_ready = sem("hot_ready")
        wall_ps = sem("wall_ps")
        prod_e = sem("prod_e")
        ehid_hi = sem("ehid_hi")
        ehid_ready = sem("ehid_ready")
        fin_copy = sem("fin_copy")
        fin_out = sem("fin_out")
        fg_in = sem("fg_in")
        stored = sem("stored")

        U = FIRST
        (O_MIX, O_MEM, O_CONV, O_Y, O_X, O_XO, O_FFN, O_2, O_MIX2, O_PEER) = range(10)
        FIRST_USE = [U[n] for n in ("uconv", "xk", "pw", "wout", "xq", "xo", "ffn", "ua", "wout2", "wq2")]
        FROM_PSUM = (O_XO, O_MIX2)
        READY = [KC * (k + 1 - sum(f < k for f in FROM_PSUM)) for k in range(10)]

        uses, filled, base = [0] * 8, {}, {}

        def emptied(eng, name):
            b, n = filled[name]
            eng.wait_ge(bank_free[b], n)

        block = ctx.enter_context(nc.Block())

        @block.sync
        def _(sp):
            def load(u, slot, guarded):
                if guarded:
                    sp.wait_ge(lo_ready, u - RING + 1)
                src = stream[u] if isinstance(u, int) else stream[bass.ds(u, 1)].rearrange("a p n -> p (a n)")
                sp.dma_start(raw[:, slot, :], src).then_inc(landed[slot], 16)

            for u in range(RING):
                load(u, u, False)
            body = (UNITS - RING) // RING
            with sp.Fori(0, body) as i:
                for s in range(RING):
                    load(i * RING + (RING + s), s, True)
            for u in range(RING * (body + 1), UNITS):
                load(u, u % RING, True)
            for t in range(TT):
                sp.wait_ge(fin_out, t + 1)
                sp.dma_start(out_d[t * P:(t + 1) * P, :], fin[:, t, :]).then_inc(stored, 16)
            sp.wait_ge(stored, 16 * TT)

        @block.tensor
        def _(pe):
            def take(b, name=None):
                if uses[b]:
                    pe.wait_ge(bank_free[b], uses[b])
                uses[b] += 1
                if name is not None:
                    filled[name] = (b, uses[b])

            def drained(*banks):
                for b in banks:
                    pe.wait_ge(bank_free[b], uses[b])

            def unit(u):
                pe.wait_ge(lo_ready, u + 1)

            def three(out, wh, wl, xh, xl, start, stop, **kw):
                pe.matmul(out, wh, xh, start=start, stop=False, **kw)
                pe.matmul(out, wh, xl, start=False, stop=False, **kw)
                return pe.matmul(out, wl, xh, start=False, stop=stop, **kw)

            def project_cols(u, b, name=None):
                s = u % RING
                unit(u)
                take(b, name)
                for c in range(KC):
                    c0 = slice(c * P, (c + 1) * P)
                    m = three(bank[b][:, 0:S], w_hi[:, s, c0], w_lo[:, s, c0], a_hi[:, c, :], a_lo[:, c, :],
                              c == 0, c == KC - 1)
                m.then_inc(unit_done, 1)

            def project_rows(u0, b, name):
                for t in range(TT):
                    take(b + t, (name, t))
                for j in range(4):
                    s = (u0 + j) % RING
                    unit(u0 + j)
                    for k in range(2):
                        c = 2 * j + k
                        n0 = slice(k * 512, (k + 1) * 512)
                        for t in range(TT):
                            t0 = slice(t * P, (t + 1) * P)
                            o = bank[b + t][:, :]
                            pe.matmul(o, a_hi[:, c, t0], w_hi[:, s, n0], start=c == 0, stop=False)
                            pe.matmul(o, a_hi[:, c, t0], w_lo[:, s, n0], start=False, stop=False)
                            m = pe.matmul(o, a_lo[:, c, t0], w_hi[:, s, n0], start=False, stop=c == KC - 1)
                    m.then_inc(unit_done, 1)

            def operand(k):
                if k in FROM_PSUM:
                    drained(4, 5, 6, 7)
                else:
                    pe.wait_ge(opnd_ready, READY[k])

            def norm(k, ready=None):
                pe.wait_ge(norm_sq, k + 1)
                take(3, ("norm", k))
                for c in range(KC):
                    m = pe.matmul(bank[3][:, 0:S], ones[:], sq[:, c, :], start=c == 0, stop=c == KC - 1)
                m.then_inc(norm_sum, 1)

            pe.wait_ge(onehot_in, 32)
            take(2, "brow")
            pe.matmul(bank[2][0:NH, :], relb[0:32], onehot[0:32], start=True, stop=True).then_inc(brow_done, 1)
            pe.wait_ge(init, 2)
            norm(0)
            operand(O_MIX)
            cj = 0
            for name in ("uconv", "q", "kc", "vc", "ks", "kw"):
                for n in range(dict(STAGES)[name]):
                    project_cols(U[name] + n, 4 + cj % 4, (name, n))
                    cj += 1
            project_rows(U["v"], 0, "v")
            u = U["gates"]
            unit(u)
            for t in range(TT):
                t0 = slice(t * P, (t + 1) * P)
                take(2 + t, ("gates", t))
                for c in range(KC):
                    n0 = slice(c * P, c * P + 3 * NH)
                    o, s = bank[2 + t][:, 0:3 * NH], u % RING
                    pe.matmul(o, a_hi[:, c, t0], w_hi[:, s, n0], start=c == 0, stop=False)
                    pe.matmul(o, a_hi[:, c, t0], w_lo[:, s, n0], start=False, stop=False)
                    m = pe.matmul(o, a_lo[:, c, t0], w_hi[:, s, n0], start=False, stop=c == KC - 1)
            m.then_inc(unit_done, 1)
            for name in ("gconv", "gattn"):
                for n in range(8):
                    project_cols(U[name] + n, 4 + cj % 4, (name, n))
                    cj += 1
            pe.wait_ge(w1_in, 16 * 12)
            for kv in range(2):
                pe.wait_ge(z_ready, kv + 1)
                take(kv)
                for l in range(CMP_BLOCK):
                    m = pe.matmul(bank[kv][:, 0:2 * NCMP], w1[kv][:, l, :], z[kv][:, l, :, :].rearrange("p a b -> p (a b)"),
                                  start=l == 0, stop=l == CMP_BLOCK - 1)
                m.then_inc(cmp_h, 1)
            drained(0)
            take(2, "kcmp")
            pe.matmul(bank[2][:, 0:2 * NCMP], w2[:, 0, :], cmid[:, 0, :], start=True, stop=True).then_inc(cmp_o, 1)
            drained(1)
            take(3, "vcmp")
            for g2 in range(2):
                m = pe.matmul(bank[3][0:NCMP, g2 * P:(g2 + 1) * P], cmid[:, 1, g2 * NCMP:(g2 + 1) * NCMP], w2[:, 1, :],
                              start=True, stop=True)
            m.then_inc(cmp_o, 1)
            operand(O_MEM)
            for n in range(8):
                project_cols(U["xk"] + n, 4 + cj % 4, ("xk", n))
                cj += 1
            project_rows(U["xv"], 0, "xv0")
            project_rows(U["xv"] + 4, 2, "xv1")
            drained(*range(8))

            def head(hh):
                c, s = hh // 2, hh % 2
                return c, slice(s * HD, (s + 1) * HD), 2 * (c // 4) + s, c // 4

            def nsa_scores(hh):
                c, r, g, gp = head(hh)
                for b, kT in enumerate((ksT, kwT)):
                    take(b, ("s", b, hh))
                    pe.matmul(bank[b][:, 0:P], qT[r, c, 0:P], kT[r, gp, 0:P], start=True, stop=True)
                    pe.matmul(bank[b][:, P:3 * P], qT[r, c, P:S], kT[r, gp, :], start=True, stop=True)
                b = 6 + hh % 2
                take(b, ("sc", hh))
                for t in range(TT):
                    m = pe.matmul(bank[b][:, 256 + t * NCMP:256 + (t + 1) * NCMP], qT[r, c, t * P:(t + 1) * P],
                                  kcmp[r, gp * NCMP:(gp + 1) * NCMP], start=True, stop=True)
                m.then_inc(scores, 1)

            def nsa_transposes(hh):
                s = hh % 2
                pe.wait_ge(scaled, hh + 1)
                for b in range(2):
                    take(2 + b)
                    for n, src in enumerate((0, 1, 2)):
                        pe.transpose(bank[2 + b][:, n * P:(n + 1) * P], prob[:, s, 384 * b + src * P:384 * b + (src + 1) * P], ident[:])
                for t in range(TT):
                    m = pe.transpose(bank[6 + s][0:NCMP, t * P:(t + 1) * P], prob[:, s, 768 + t * NCMP:768 + (t + 1) * NCMP], ident[:])
                m.then_inc(probsT, 1)

            def nsa_values(hh):
                c, r, g, gp = head(hh)
                s = hh % 2
                if s == 0:
                    take(4 + c % 2, ("o", c))
                o = bank[4 + c % 2]
                drained(2, 3, 6 + s)
                for b in range(2):
                    v0 = slice(b * 256 + g * HD, b * 256 + (g + 1) * HD)
                    pe.matmul(o[r, 0:S], vrows[:, 0, v0], pT[:, b, 0:S], start=b == 0, stop=False, skip_group_check=True)
                    pe.matmul(o[r, P:S], vrows[:, 1, v0], pT[:, b, S:S + P], start=False, stop=False, skip_group_check=True)
                pe.matmul(o[r, 0:S], vcmp[0:NCMP, gp, r], pcT[0:NCMP, s, :], start=False, stop=True,
                          skip_group_check=True).then_inc(attended, 1)

            nsa_scores(0)
            for hh in range(NH):
                if hh + 1 < NH:
                    nsa_scores(hh + 1)
                nsa_transposes(hh)
                nsa_values(hh)
            pe.wait_ge(taps, KC * CONV_W)
            take(0, "cmean")
            for c in range(KC):
                m = pe.matmul(bank[0][:, 0:S], ones[:], cacc[:, c, :], start=c == 0, stop=c == KC - 1)
            m.then_inc(conv_sum, 1)
            pe.wait_ge(conv_cent, 1)
            take(1, "cvar")
            for c in range(KC):
                m = pe.matmul(bank[1][:, 0:S], ones[:], hf[:, c, :], start=c == 0, stop=c == KC - 1)
            m.then_inc(conv_var, 1)
            for k, name in ((O_CONV, "pw"), (O_Y, "wout")):
                operand(k)
                for n in range(8):
                    project_cols(U[name] + n, 4 + cj % 4, (name, n))
                    cj += 1
            norm(1)
            operand(O_X)
            for n in range(8):
                project_cols(U["xq"] + n, 4 + cj % 4, ("xq", n))
                cj += 1

            def x_scores(h):
                take(h % 2, ("xs", h))
                for t in range(TT):
                    for k in range(2):
                        m = pe.matmul(bank[h % 2][:, t * S:(t + 1) * S], qT[:, 2 * h + k, t * P:(t + 1) * P],
                                      kx[:, 2 * h + k, :], start=k == 0, stop=k == 1)
                m.then_inc(xs, 1)

            drained(4, 5, 6, 7)
            x_scores(0)
            for h in range(XH):
                if h + 1 < XH:
                    x_scores(h + 1)
                s = h % 2
                pe.wait_ge(xs_scaled, h + 1)
                take(2 + s, ("xpt", h))
                for kt in range(2):
                    for t in range(TT):
                        m = pe.transpose(bank[2 + s][:, kt * S + t * P:kt * S + (t + 1) * P],
                                         xprob[:, s, t * S + kt * P:t * S + (kt + 1) * P], ident[:])
                m.then_inc(xpt, 1)
                drained(2 + s)
                for k in range(2):
                    b = 4 + cj % 4
                    cj += 1
                    take(b, ("xo_in", 2 * h + k))
                    d0 = h * XHD + k * P
                    for kt in range(2):
                        m = pe.matmul(bank[b][:, 0:S], vx[:, kt, d0:d0 + P], xpT[:, s, kt * S:(kt + 1) * S],
                                      start=kt == 0, stop=kt == 1)
                    m.then_inc(xo_done, 1)
            operand(O_XO)
            for n in range(8):
                project_cols(U["xo"] + n, 4 + cj % 4, ("xo", n))
                cj += 1
            norm(2)
            for b in range(4):
                take(b, ("ffn", b))
                for k in range(2):
                    pe.matmul(bank[b][:, k * S:(k + 1) * S], ident[:], xT[:, 2 * b + k, :], start=k == 0, stop=False,
                              skip_group_check=True)
            operand(O_FFN)

            def ffn_up(u, slot, b, free):
                pe.wait_ge(lo_ready, u + 1)
                if free is not None:
                    pe.wait_ge(bank_free[b], free)
                for c in range(KC):
                    c0 = slice(c * P, (c + 1) * P)
                    m = three(bank[b][:, 0:S], w_hi[:, slot, c0], w_lo[:, slot, c0], a_hi[:, c, :], a_lo[:, c, :],
                              c == 0, c == KC - 1)
                m.then_inc(unit_done, 1)

            def ffn_down(u, slot, f, par, last=False):
                pe.wait_ge(lo_ready, u + 1)
                pe.wait_ge(hid_ready, f + 1)
                for c in range(KC):
                    c0 = slice(c * P, (c + 1) * P)
                    m = three(bank[c // 2][:, (c % 2) * S:(c % 2 + 1) * S], w_hi[:, slot, c0], w_lo[:, slot, c0],
                              h_hi[:, par, :], h_lo[:, par, :], False, last, skip_group_check=True)
                m.then_inc(unit_done, 1)

            u0 = U["ffn"]
            base["ffn"] = uses[4:8]
            ffn_up(u0, u0 % RING, 4, uses[4])
            ffn_up(u0 + 1, (u0 + 1) % RING, 5, uses[5])
            with pe.Fori(0, 5) as i:
                for k in range(4):
                    b = 4 + 2 * ((k + 1) % 2)
                    for n in range(2):
                        had = uses[b + n] + (1 if (k + 1) % 2 == 0 else 0) + k // 2
                        ffn_up(i * 12 + (u0 + 2 + 3 * k + n), (u0 + 2 + 3 * k + n) % RING, b + n, i * 2 + had)
                    ffn_down(i * 12 + (u0 + 4 + 3 * k), (u0 + 4 + 3 * k) % RING, i * 4 + k, k % 2)
            f = FC - 1
            u = u0 + 2 + 3 * (f - 1)
            for n in range(2):
                ffn_up(u + n, (u + n) % RING, 6 + n, uses[6 + n] + f // 2)
            for b in (4, 5, 6, 7):
                uses[b] += FC // 2
            ffn_down(u + 2, (u + 2) % RING, f - 1, (f - 1) % 2)
            ffn_down(u + 3, (u + 3) % RING, f, f % 2, last=True)
            norm(3)
            norm(4)
            operand(O_2)
            for n, name in enumerate(("ua", "va", "q2", "k2", "v2")):
                project_rows(U[name], 2 * (n % 2), name)
            pe.wait_ge(ln2, TT)
            pe.wait_ge(const2_in, 64)
            for t in range(TT):
                take(4 + t, ("mixed", t))
                for g in range(8):
                    m = pe.matmul(bank[4 + t][:, g * 64:(g + 1) * 64], wsT[:, g, :], va[:, t, g * 64:(g + 1) * 64],
                                  start=True, stop=True)
                m.then_inc(mixed, 1)
            for n in range(2):
                pe.wait_ge(roped, n + 1)
                for half in range(2):
                    take(6 + half, ("qk", n, half))
                    for j in range(2):
                        c = 2 * half + j
                        for t in range(TT):
                            src = (q2, k2)[n][:, t, c * P:(c + 1) * P]
                            m = pe.transpose(bank[6 + half][:, j * S + t * P:j * S + (t + 1) * P], src, ident[:])
                    m.then_inc(qk_t, 1)
            drained(0, 1, 6, 7)

            def scores2(h):
                r, c, b = slice((h % 2) * HD2, (h % 2 + 1) * HD2), h // 2, h % 2
                take(b, ("s2", h))
                for t in range(TT):
                    m = pe.matmul(bank[b][:, t * S:(t + 1) * S], qk2T[r, 0, c, t * P:(t + 1) * P], qk2T[r, 1, c, :],
                                  start=True, stop=True)
                m.then_inc(s2, 1)

            scores2(0)
            for h in range(H2):
                if h + 1 < H2:
                    scores2(h + 1)
                s = h % 2
                pe.wait_ge(s2_exp, h + 1)
                take(2 + s, ("p2t", h))
                for kt in range(2):
                    for t in range(TT):
                        m = pe.transpose(bank[2 + s][:, kt * S + t * P:kt * S + (t + 1) * P],
                                         prob2[:, s, t * S + kt * P:t * S + (kt + 1) * P], ident[:])
                m.then_inc(p2t, 1)
                drained(2 + s)
                take(4 + s, ("o2", h))
                for t in range(TT):
                    for kt in range(2):
                        m = pe.matmul(bank[4 + s][:, t * HD2:(t + 1) * HD2], pT2[:, s, kt * S + t * P:kt * S + (t + 1) * P],
                                      v2[:, kt, h * HD2:(h + 1) * HD2], start=kt == 0, stop=kt == 1)
                m.then_inc(o2, 1)
            pe.wait_ge(mix_ready, 2 * TT)
            for c in range(KC):
                b = 4 + cj % 4
                cj += 1
                take(b, ("mixT", c))
                for t in range(TT):
                    m = pe.transpose(bank[b][:, t * P:(t + 1) * P], mix[:, c // 4, t, (c % 4) * P:(c % 4 + 1) * P], ident[:])
                m.then_inc(mix_t, 1)
            operand(O_MIX2)
            for n in range(8):
                project_cols(U["wout2"] + n, 4 + cj % 4, ("wout2", n))
                cj += 1
            norm(5)
            operand(O_PEER)
            for n in range(16):
                project_cols(U["wq2"] + n, 4 + cj % 4, ("wq2", n))
                cj += 1
            pe.wait_ge(const2_in, 96)
            drained(4, 5, 6, 7)
            for t in range(TT):
                for n in range(4):
                    b = n % 4
                    take(b, ("sk", t, n))
                    for j in range(4):
                        hp = 4 * n + j
                        m = pe.matmul(bank[b][:, j * NK:(j + 1) * NK], qq[:, hp, t * P:(t + 1) * P], skT[:, hp % 2, :],
                                      start=True, stop=True)
                    m.then_inc(sk_s, 1)
            for t in range(TT):
                pe.wait_ge(routed, t + 1)
                take(4 + t, ("route", t))
                for n in range(3):
                    m = pe.transpose(bank[4 + t][:, n * P:(n + 1) * P], pick[:, n, t, :], ident[:])
                m.then_inc(route_t, 1)
            drained(4, 5)
            for t in range(TT):
                for half in range(2):
                    b = 2 * t + half
                    take(b)
                    for j in range(4):
                        m = pe.matmul(bank[b][:, j * P:(j + 1) * P], xT[:, 4 * half + j, t * P:(t + 1) * P], ident[:],
                                      start=j == 0, stop=False, skip_group_check=True)
                m.then_inc(wall_ps, 1)
            for b in (4, 5):
                uses[b] += 1
            base["wall"] = uses[4:6]
            with pe.Fori(0, S // 8) as i:
                for q in range(2):
                    pe.wait_ge(bank_free[4 + q], i + (uses[4 + q] - 1))
                    for j in range(4):
                        n = 4 * q + j
                        pair, k = n // 2, n % 2
                        if k == 0:
                            pe.wait_ge(hot_ready, i * 4 + (pair + 1))
                        m = pe.matmul(bank[4 + q][:, j * P:(j + 1) * P], hot[:, pair % 2, k, 1, :], hot[:, pair % 2, k, 0, :],
                                      start=True, stop=True)
                        if k == 1:
                            m.then_inc(wall_ps, 1)
            for b in (4, 5):
                uses[b] += S // 8 - 1
            def expert_up(u, slot, b, free):
                pe.wait_ge(lo_ready, u + 1)
                pe.wait_ge(bank_free[b], free)
                for c in range(KC):
                    c0 = slice(c * P, (c + 1) * P)
                    m = three(bank[b][:, 0:S], w_hi[:, slot, c0], w_lo[:, slot, c0], a_hi[:, c, :], a_lo[:, c, :],
                              c == 0, c == KC - 1)
                m.then_inc(unit_done, 1)

            def expert_down(u, slot, n, par, last=False):
                pe.wait_ge(lo_ready, u + 1)
                pe.wait_ge(ehid_ready, n + 1)
                for t in range(TT):
                    t0 = slice(t * P, (t + 1) * P)
                    for half in range(2):
                        n0 = slice(half * 512, (half + 1) * 512)
                        o = bank[2 * t + half][:, :]
                        pe.matmul(o, h_hi[:, par, t0], w_hi[:, slot, n0], start=False, stop=False, skip_group_check=True)
                        pe.matmul(o, h_hi[:, par, t0], w_lo[:, slot, n0], start=False, stop=False, skip_group_check=True)
                        m = pe.matmul(o, h_lo[:, par, t0], w_hi[:, slot, n0], start=False, stop=last, skip_group_check=True)
                m.then_inc(unit_done, 1)

            u0 = U["experts"]
            base["experts"] = uses[4:6]
            expert_up(u0, u0 % RING, 4, uses[4])
            with pe.Fori(0, NEXP // 2 - 1) as i:
                for k in range(2):
                    b = 4 + (k + 1) % 2
                    had = uses[b] + (1 if k == 1 else 0)
                    u = u0 + 1 + 2 * k
                    expert_up(i * 4 + u, u % RING, b, i + had)
                    expert_down(i * 4 + (u + 1), (u + 1) % RING, i * 2 + k, k % 2)
            n = NEXP - 1
            u = u0 + 1 + 2 * (n - 1)
            expert_up(u, u % RING, 5, uses[5] + n // 2)
            expert_down(u + 1, (u + 1) % RING, n - 1, (n - 1) % 2)
            expert_down(u + 2, (u + 2) % RING, n, n % 2, last=True)

        @block.gpsimd
        def _(pool):
            pool.dma_start(xT, xT_d).then_inc(x_in, 16)
            pool.dma_start(ident[:], ident_d).then_inc(consts_in, 16)
            pool.dma_start(cols[:], cols_d).then_inc(consts_in, 16)
            pool.dma_start(onehot[0:32], onehot_d).then_inc(onehot_in, 16)
            pool.dma_start(relb[0:32], relb_d).then_inc(onehot_in, 16)
            pool.dma_start(dw, dw_d).then_inc(consts_in, 16)
            pool.memset(ones[:], 1.0 / D).then_inc(init, 1)
            pool.memset(eps[:], EPS).then_inc(init, 1)
            pool.memset(vconv[:, :, 0:CONV_W - 1], 0.0).then_inc(init, 1)
            for w in (w1[0], w1[1], w2):
                pool.memset(w, 0.0).then_inc(pool_seq, 1)
            pool.wait_ge(pool_seq, 3)
            for kv in range(2):
                for half in range(2):
                    r = slice(half * HD, (half + 1) * HD)
                    pool.dma_start(w1[kv][r, :, r], w1_d[kv]).then_inc(w1_in, 16)
                    pool.dma_start(w2[r, kv, r], w2_d[kv]).then_inc(w1_in, 16)
                    pool.dma_start(pos[r, kv, :], pos_d[kv]).then_inc(w1_in, 16)
            emptied(pool, "brow")
            pool.wait_ge(brow_sb, 1)
            pool.dma_start(bias_d.ap(), brow[0:NH].unsqueeze(1).to_broadcast([NH, P, 512])).then_inc(brow_out, 16)
            pool.wait_ge(brow_out, 16)
            pool.wait_ge(opnd_ready, READY[O_MIX])
            pool.dma_start(hf, memT_d).then_inc(mem_in, 16)
            pool.wait_ge(cmp_o, 2)
            for h in range(NH):
                pool.dma_start(bias[:, h, :], bass.AP(bias_d, h * P * 512 + P - 1, [[511, P], [1, 384]])).then_inc(bias_in, 16)
            for hh in range(NH):
                s = hh % 2
                pool.wait_ge(scale_ready, hh + 1)
                pool.wait_ge(exped, hh + 1)
                for b in range(3):
                    for t in range(TT):
                        n0, n1 = [(0, P), (P, 384)][t] if b < 2 else (t * NCMP, (t + 1) * NCMP)
                        v = prob[:, s, 384 * b + n0:384 * b + n1]
                        ins = pool.tensor_scalar(v, v, rinv[:, s, 2 * b + t:2 * b + t + 1], 1.0, ALU.mult, ALU.mult)
                ins.then_inc(scaled, 1)
            for h in range(XH):
                pool.wait_ge(xs_rinv, h + 1)
                emptied(pool, ("xs", h))
                for t in range(TT):
                    v = xprob[:, h % 2, t * S:(t + 1) * S]
                    ins = pool.tensor_scalar(v, v, rinv[:, h % 2, t:t + 1], 1.0, ALU.mult, ALU.mult)
                ins.then_inc(xs_scaled, 1)
            pool.wait_ge(norm_sum, 3)
            for dst, src in ((wsT, wsT_d), (rope, rope_d), (bs, bs_d), (lc, lc_d)):
                pool.dma_start(dst, src).then_inc(const2_in, 16)
            for n in range(2):
                pool.dma_start(lnv[:, n, :], lnv_d[n:n + 1, :].to_broadcast([P, 512])).then_inc(lnv_in, 16)
            pool.wait_ge(norm_sum, 6)
            pool.dma_start(skT, skT_d).then_inc(const2_in, 16)
            pool.dma_start(iota, iota_d).then_inc(const2_in, 16)
            pool.wait_ge(fin_copy, 1)
            pool.dma_start(fg, fg_d.to_broadcast([P, D])).then_inc(fg_in, 16)

        @block.scalar
        def _(act):
            rounded, seq = [0], [0]

            def hi(u, slot):
                act.wait_ge(landed[slot], (u - slot) * (16 // RING) + 16)
                if not isinstance(u, int) or u >= RING:
                    act.wait_ge(unit_done, u - RING + 1)
                act.activation(w_hi[:, slot, :], raw[:, slot, :], ACT.Copy).then_inc(hi_ready, 1)

            def hi_to(n):
                for u in range(rounded[0], min(n, UNITS)):
                    hi(u, u % RING)
                rounded[0] = max(rounded[0], n)

            def after(ins):
                ins.then_inc(act_seq, 1)
                seq[0] += 1
                act.wait_ge(act_seq, seq[0])

            def from_unit(u):
                hi_to(u + RING)
                act.wait_ge(unit_done, u + 1)

            def copy_cols(name, n, dst, scale=1.0, func=ACT.Copy):
                from_unit(U[name] + n)
                b, _ = filled[(name, n)]
                act.activation(dst, bank[b][:, 0:S], func, scale=scale).then_inc(bank_free[b], 1)

            def copy_rows(name, first, dst, scale=1.0, func=ACT.Copy):
                from_unit(first + 3)
                for t in range(TT):
                    b, _ = filled[(name, t)]
                    act.activation(dst[t], bank[b][:, :], func, scale=scale).then_inc(bank_free[b], 1)

            def norm(k):
                act.wait_ge(norm_sum, k + 1)
                if k:
                    act.wait_ge(norm_out, KC * k)
                act.activation(std[:], bank[3][:, 0:S], ACT.Sqrt, bias=eps[:, 0:1]).then_inc(bank_free[3], 1)

            def operand(k, source, ready, first=0, scale=None):
                hi_to(FIRST_USE[k] + RING - 1)
                act.wait_ge(unit_done, FIRST_USE[k]) if FIRST_USE[k] else None
                for c in range(KC):
                    ready(c)
                    act.activation(a_hi[:, c, :], source(c), ACT.Copy, scale=1.0 if scale is None else scale(c))\
                       .then_inc(opnd_hi, 1)

            def normed_operand(k, n):
                operand(k, lambda c: hf[:, c, :], lambda c: act.wait_ge(norm_out, KC * n + c + 1))

            def row_std(v, n):
                act.wait_ge(stat_ready, n)
                act.activation(v, v, ACT.Sqrt, bias=eps[:, 0:1]).then_inc(stat_std, 1)

            hi_to(RING)
            act.wait_ge(brow_done, 1)
            act.activation(brow[0:NH, 0:S], bank[2][0:NH, 0:S], ACT.Copy).then_inc(bank_free[2], 1)
            act.wait_ge(init, 2)
            norm(0)
            act.wait_ge(consts_in, 48)
            normed_operand(O_MIX, 0)
            for j in range(KC):
                from_unit(U["uconv"] + 2 * j + 1)
                if j >= 2:
                    emptied(act, ("uconv", 2 * (j - 2)))
                b, _ = filled[("uconv", 2 * j + 1)]
                act.activation(act2[:, j % 2, :], bank[b][:, 0:S], ACT.Sigmoid).then_inc(bank_free[b], 1)
            for j in range(8):
                copy_cols("q", j, qT[:, j, :], scale=HD ** -0.5)
            for name, dst in (("kc", kcT), ("vc", vcT), ("ks", ksT), ("kw", kwT)):
                for j in range(2):
                    copy_cols(name, j, dst[:, j, :])
            copy_rows("v", U["v"], [vrows[:, t, :] for t in range(TT)])
            from_unit(U["gates"])
            for t in range(TT):
                b, _ = filled[("gates", t)]
                act.activation(gates[:, :, :, t], bank[b][:, 0:3 * NH].rearrange("p (b h) -> p b h", b=3), ACT.Sigmoid)\
                   .then_inc(bank_free[b], 1)
            for name, dst in (("gconv", gcon), ("gattn", gatt)):
                for j in range(8):
                    copy_cols(name, j, dst[:, j, :], func=ACT.Sigmoid)
            for kv in range(2):
                act.wait_ge(cmp_h, kv + 1)
                act.activation(cmid[:, kv, :], bank[kv][:, 0:2 * NCMP], ACT.Silu).then_inc(bank_free[kv], 1)
            act.wait_ge(cmp_o, 1)
            act.activation(kcmp, bank[2][:, 0:2 * NCMP], ACT.Copy).then_inc(bank_free[2], 1)
            act.wait_ge(cmp_o, 2)
            act.activation(vcmp[0:NCMP], bank[3][0:NCMP, 0:2 * P].rearrange("p (a b) -> p a b", a=2), ACT.Copy)\
               .then_inc(bank_free[3], 1)
            operand(O_MEM, lambda c: hf[:, c, :], lambda c: act.wait_ge(mem_in, 16))
            for j in range(8):
                copy_cols("xk", j, kx[:, j, :])
            for half in range(2):
                copy_rows(f"xv{half}", U["xv"] + 4 * half, [vx[:, t, half * 512:(half + 1) * 512] for t in range(TT)])
            def nsa_exp(hh):
                s = hh % 2
                act.wait_ge(biased, hh + 1)
                for b in range(3):
                    for t in range(TT):
                        n0, n1 = [(0, P), (P, 384)][t] if b < 2 else (t * NCMP, (t + 1) * NCMP)
                        v = prob[:, s, 384 * b + n0:384 * b + n1]
                        k = 2 * b + t
                        ins = act.activation(v, v, ACT.Exp, bias=mx[:, s, k:k + 1], accum_out=sums[:, s, k:k + 1])
                ins.then_inc(exped, 1)

            nsa_exp(0)
            for hh in range(NH):
                if hh + 1 < NH:
                    nsa_exp(hh + 1)
                act.wait_ge(probsT, hh + 1)
                if hh:
                    act.wait_ge(attended, hh)
                act.activation(pT[:, 0, 0:384], bank[2][:, 0:384], ACT.Copy).then_inc(bank_free[2], 1)
            act.wait_ge(conv_var, 1)
            act.activation(std[:], bank[1][:, 0:S], ACT.Sqrt, bias=eps[:, 0:1]).then_inc(bank_free[1], 1)
            for c in range(KC):
                act.wait_ge(conv_ln, c + 1)
                act.activation(sq[:, c, :], hf[:, c, :], ACT.Silu, bias=cols[:, CONV_LNB, c:c + 1]).then_inc(conv_act, 1)
            operand(O_CONV, lambda c: sq[:, c, :], lambda c: act.wait_ge(conv_act, c + 1))
            hi_to(U["wout"] + RING - 1)
            operand(O_Y, lambda c: hf[:, c, :], lambda c: act.wait_ge(y_ready, c + 1))
            hi_to(U["xq"] + RING - 1)
            norm(1)
            normed_operand(O_X, 1)
            for j in range(8):
                copy_cols("xq", j, qT[:, j, :], scale=XHD ** -0.5)

            def x_exp(h):
                s = h % 2
                act.wait_ge(xs_max, h + 1)
                if h >= 2:
                    act.wait_ge(xpt, h - 1)
                for t in range(TT):
                    ins = act.activation(xprob[:, s, t * S:(t + 1) * S], bank[s][:, t * S:(t + 1) * S], ACT.Exp,
                                         bias=mx[:, s, t:t + 1], accum_out=sums[:, s, t:t + 1])
                ins.then_inc(bank_free[s], 1)

            hi_to(U["xo"] + RING - 1)
            x_exp(0)
            for h in range(XH):
                s = h % 2
                if h + 1 < XH:
                    x_exp(h + 1)
                act.wait_ge(xpt, h + 1)
                if h >= 2:
                    act.wait_ge(xo_done, 2 * (h - 1))
                act.activation(xpT[:, s, :], bank[2 + s][:, :], ACT.Copy).then_inc(bank_free[2 + s], 1)
                for k in range(2):
                    c = 2 * h + k
                    act.wait_ge(xo_done, c + 1)
                    b, _ = filled[("xo_in", c)]
                    act.activation(a_hi[:, c, :], bank[b][:, 0:S], ACT.Copy).then_inc(opnd_hi, 1)
            hi_to(U["ffn"] + RING - 1)
            norm(2)
            normed_operand(O_FFN, 2)
            u0 = U["ffn"]

            def ffn_act(u, k, par, f, n):
                b = 4 + 2 * par
                act.wait_ge(unit_done, u + 1)
                if f is not None:
                    act.wait_ge(hid_ready, f)
                act.activation(act2[:, par, :], bank[b][:, 0:S], ACT.Silu).then_inc(bank_free[b], 1)

            def ffn_hi(par, n, k):
                act.wait_ge(bank_free[5 + 2 * par], n)
                act.activation(h_hi[:, par, :], act2[:, par, :], ACT.Copy).then_inc(hid_hi, 1)

            n0 = base["ffn"]
            hi(u0 + RING - 1, (u0 + RING - 1) % RING)
            ffn_act(u0, 0, 0, None, 0)
            ffn_hi(0, n0[1] + 1, 0)
            hi(u0 + RING, (u0 + RING) % RING)
            with act.Fori(0, 5) as i:
                for k in range(4):
                    u, par = u0 + 2 + 3 * k, (k + 1) % 2
                    hi(i * 12 + (u + 3), (u + 3) % RING)
                    ffn_act(i * 12 + u, k, par, i * 4 + (k + 1), 0)
                    hi(i * 12 + (u + 4), (u + 4) % RING)
                    ffn_hi(par, i * 2 + (n0[1 + 2 * par] + 1 + (k + 1) // 2), k)
                    hi(i * 12 + (u + 5), (u + 5) % RING)
            f = FC - 1
            u = u0 + 2 + 3 * (f - 1)
            rounded[0] = u + 3
            hi_to(u + RING)
            ffn_act(u, 0, 1, f, 0)
            hi_to(u + 1 + RING)
            ffn_hi(1, n0[3] + 1 + f // 2, 0)
            hi_to(U["ua"] + RING - 1)
            norm(3)
            norm(4)
            normed_operand(O_2, 4)
            copy_rows("ua", U["ua"], [ua[:, t, :] for t in range(TT)], func=ACT.Gelu_apprx_tanh)
            copy_rows("va", U["va"], [va[:, t, :] for t in range(TT)], func=ACT.Gelu_apprx_tanh)
            copy_rows("q2", U["q2"], [q2[:, t, :] for t in range(TT)], scale=HD2 ** -0.5)
            row_std(stat[:, 0:4].rearrange("p (t a) -> p t a", a=2)[:, :, 1], TT)
            copy_rows("k2", U["k2"], [k2[:, t, :] for t in range(TT)])
            copy_rows("v2", U["v2"], [v2[:, t, :] for t in range(TT)])
            for n in range(2):
                for half in range(2):
                    act.wait_ge(qk_t, 2 * n + half + 1)
                    act.activation(qk2T[:, n, 2 * half:2 * half + 2, :].rearrange("p a b -> p (a b)"), bank[6 + half][:, :],
                                   ACT.Copy).then_inc(bank_free[6 + half], 1)

            def exp2(h):
                s = h % 2
                act.wait_ge(s2_biased, h + 1)
                for t in range(TT):
                    v = prob2[:, s, t * S:(t + 1) * S]
                    ins = act.activation(v, v, ACT.Exp, bias=mx[:, s, t:t + 1], accum_out=sums[:, s, t:t + 1])
                ins.then_inc(s2_exp, 1)

            exp2(0)
            for h in range(H2):
                s = h % 2
                if h + 1 < H2:
                    exp2(h + 1)
                act.wait_ge(p2t, h + 1)
                if h >= 2:
                    act.wait_ge(o2, h - 1)
                act.activation(pT2[:, s, :], bank[2 + s][:, :], ACT.Copy).then_inc(bank_free[2 + s], 1)
            row_std(stat[:, 4:8], TT + 1)
            for c in range(KC):
                act.wait_ge(mix_t, c + 1)
                b, _ = filled[("mixT", c)]
                act.activation(a_hi[:, c, :], bank[b][:, 0:S], ACT.Copy, scale=cols[:, G_OUT2, c:c + 1]).then_inc(opnd_hi, 1)
            hi_to(U["wq2"] + RING - 1)
            norm(5)
            normed_operand(O_PEER, 5)
            for j in range(16):
                copy_cols("wq2", j, qq[:, j, :])
            for t in range(TT):
                for n in range(4):
                    act.wait_ge(sk_s, 4 * t + n + 1)
                    b, _ = filled[("sk", t, n)]
                    act.activation(sc[:, t, 4 * n:4 * n + 4, :].rearrange("p a b -> p (a b)"), bank[b][:, :], ACT.Copy)\
                       .then_inc(bank_free[b], 1)
            act.wait_ge(c_sub, 1)
            act.activation(pick[:, 2, :, :], pick[:, 2, :, :], ACT.Exp).then_inc(c_exp, 1)
            for t in range(TT):
                act.wait_ge(route_t, t + 1)
                act.activation(routeT[:, :, t * P:(t + 1) * P], bank[4 + t][:, 0:384].rearrange("p (a b) -> p a b", a=3), ACT.Copy)\
                   .then_inc(bank_free[4 + t], 1)
            with act.Fori(0, S // 8) as i:
                for q in range(2):
                    act.wait_ge(wall_ps, i * 4 + (2 + 2 * q + 2))
                    act.activation(wall[:, :, bass.ds(i * 8 + 4 * q, 4)].rearrange("p i t -> p t i"),
                                   bank[4 + q][:, :].rearrange("p (t i) -> p t i", t=4), ACT.Copy).then_inc(bank_free[4 + q], 1)
            u0 = U["experts"]
            n0 = base["experts"]

            def expert_gelu(u, par, n):
                act.wait_ge(unit_done, u + 1)
                if n is not None:
                    act.wait_ge(ehid_ready, n)
                act.activation(act2[:, par, :], bank[4 + par][:, 0:S], ACT.Gelu_apprx_tanh).then_inc(bank_free[4 + par], 1)

            def expert_hi(par, n):
                act.wait_ge(prod_e, n + 1)
                act.activation(h_hi[:, par, :], act2[:, par, :], ACT.Copy).then_inc(ehid_hi, 1)

            hi_to(u0 + RING - 1)
            expert_gelu(u0, 0, None)
            hi(u0 + 3, (u0 + 3) % RING)
            expert_hi(0, 0)
            with act.Fori(0, NEXP // 2 - 1) as i:
                for k in range(2):
                    u, par = u0 + 1 + 2 * k, (k + 1) % 2
                    hi(i * 4 + (u + 3), (u + 3) % RING)
                    expert_gelu(i * 4 + u, par, i * 2 + (k + 1))
                    hi(i * 4 + (u + 4), (u + 4) % RING)
                    expert_hi(par, i * 2 + (1 + k))
            n = NEXP - 1
            u = u0 + 1 + 2 * (n - 1)
            expert_gelu(u, 1, n)
            expert_hi(1, n)
            row_std(sums[:, 0, 0:TT], TT + 2)

        @block.vector
        def _(dve):
            split_done, seq = [0], [0]

            def lo(u, slot):
                dve.wait_ge(hi_ready, u + 1)
                dve.tensor_tensor(w_lo[:, slot, :], raw[:, slot, :], w_hi[:, slot, :].bitcast(F32), ALU.subtract)\
                   .then_inc(lo_ready, 1)

            def lo_to(n):
                for u in range(split_done[0], min(n, UNITS)):
                    lo(u, u % RING)
                split_done[0] = max(split_done[0], n)

            def after(ins):
                ins.then_inc(dve_seq, 1)
                seq[0] += 1
                dve.wait_ge(dve_seq, seq[0])

            def from_unit(u):
                lo_to(u + RING)
                dve.wait_ge(unit_done, u + 1)

            def squares(k, n):
                dve.tensor_tensor(sq, xT, xT, ALU.mult).then_inc(norm_sq, 1)

            def rstd(b_name):
                emptied(dve, b_name)
                after(dve.reciprocal(std[:], std[:]))

            def normed(n, gain, dst):
                rstd(("norm", n))
                for c in range(KC):
                    dve.scalar_tensor_tensor(dst[:, c, :], xT[:, c, :], cols[:, gain, c:c + 1], std[:], ALU.mult, ALU.mult)\
                       .then_inc(norm_out, 1)

            def operand_rest(k, source):
                lo_to(FIRST_USE[k] + RING - 1)
                h0 = KC * k
                for c in range(KC):
                    dve.wait_ge(opnd_hi, h0 + c + 1)
                    dve.tensor_tensor(a_lo[:, c, :], source(c), a_hi[:, c, :].bitcast(F32), ALU.subtract)\
                       .then_inc(opnd_ready, 1)

            def residual(name):
                for j in range(KC):
                    from_unit(U[name] + j)
                    b, _ = filled[(name, j)]
                    dve.tensor_tensor(xT[:, j, :], bank[b][:, 0:S], xT[:, j, :], ALU.add).then_inc(bank_free[b], 1)
                for j in range(KC):
                    emptied(dve, (name, j))

            dve.wait_ge(x_in, 16)
            squares(0, 0)
            lo_to(RING - 1)
            dve.wait_ge(onehot_in, 32)
            dve.memset(brow[0:NH, S:2 * S], NEG).then_inc(brow_sb, 1)
            dve.wait_ge(consts_in, 48)
            normed(0, G_MIX, hf)
            operand_rest(O_MIX, lambda c: hf[:, c, :])
            dve.wait_ge(init, 3)
            for j in range(KC):
                from_unit(U["uconv"] + 2 * j + 1)
                emptied(dve, ("uconv", 2 * j + 1))
                b, _ = filled[("uconv", 2 * j)]
                dve.tensor_tensor(vconv[:, j, CONV_W - 1:], bank[b][:, 0:S], act2[:, j % 2, :], ALU.mult)\
                   .then_inc(bank_free[b], 1)
            for j in range(KC):
                emptied(dve, ("uconv", 2 * j))
            dve.wait_ge(brow_out, 16)

            def tap(n):
                k, c = n // KC, n % KC
                v, w = vconv[:, c, k:k + S], dw[:, c, k:k + 1]
                if k == 0:
                    ins = dve.tensor_scalar(cacc[:, c, :], v, w, cols[:, CONV_B, c:c + 1], ALU.mult, ALU.add)
                else:
                    dve.wait_ge(taps, n - KC + 1)
                    ins = dve.scalar_tensor_tensor(cacc[:, c, :], v, w, cacc[:, c, :], ALU.mult, ALU.add)
                ins.then_inc(taps, 1)

            first, last = U["q"], U["pw"]
            for u in range(first, last):
                if u == U["v"]:
                    for kv, (name, off) in enumerate((("kc", 10240), ("vc", 10752))):
                        for j in range(2):
                            emptied(dve, (name, j))
                        if kv == 0:
                            dve.wait_ge(w1_in, 16 * 12)
                        blocks = bass.AP(arena, off, [[P * S, P], [1, CMP_BLOCK], [S, 2], [CMP_STRIDE, NCMP]])
                        dve.tensor_tensor(z[kv], blocks, pos[:, kv, :].unsqueeze(2).unsqueeze(3)
                                          .to_broadcast([P, CMP_BLOCK, 2, NCMP]), ALU.add).then_inc(z_ready, 1)
                if u == U["xk"]:
                    operand_rest(O_MEM, lambda c: hf[:, c, :])
                lo_to(u + RING)
                for n in range(KC * CONV_W * (u - first) // (last - first), KC * CONV_W * (u + 1 - first) // (last - first)):
                    tap(n)
            for t in range(TT):
                emptied(dve, ("gates", t))
            emptied(dve, ("gattn", 7))
            dve.wait_ge(bias_in, 16 * NH)

            def nsa_bias(hh):
                s = hh % 2
                dve.wait_ge(scores, hh + 1)
                if hh >= 2:
                    dve.wait_ge(probsT, hh - 1)
                for b in range(2):
                    for t in range(TT):
                        n0, n1 = ((0, P), (P, 384))[t]
                        ins = dve.tensor_tensor_reduce(prob[:, s, 384 * b + n0:384 * b + n1], bank[b][:, n0:n1],
                                                       bias[:, hh, P:S] if t == 0 else bias[:, hh, 0:S], 1.0, MAX_FLOOR,
                                                       ALU.add, ALU.max, mx[:, s, 2 * b + t:2 * b + t + 1])
                    ins.then_inc(bank_free[b], 1)
                for t in range(TT):
                    j0 = CMP_BLOCK - 1 + P * (1 - t)
                    ins = dve.tensor_tensor_reduce(prob[:, s, 768 + t * NCMP:768 + (t + 1) * NCMP],
                                                   bank[6 + s][:, S + t * NCMP:S + (t + 1) * NCMP],
                                                   bias[:, hh, j0:j0 + CMP_STRIDE * (NCMP - 1) + 1:CMP_STRIDE], 1.0, MAX_FLOOR,
                                                   ALU.add, ALU.max, mx[:, s, 4 + t:5 + t])
                after(ins)
                for b in range(2):
                    emptied(dve, ("s", b, hh))
                dve.tensor_scalar(mx[:, s, :], mx[:, s, :], -1.0, None, ALU.mult).then_inc(biased, 1)

            nsa_bias(0)
            for hh in range(NH):
                s, c = hh % 2, hh // 2
                if hh + 1 < NH:
                    nsa_bias(hh + 1)
                dve.wait_ge(exped, hh + 1)
                after(dve.tensor_scalar(rinv[:, s, :], sums[:, s, :], 1e-30, None, ALU.max))
                after(dve.reciprocal(rinv[:, s, :], rinv[:, s, :]))
                r3 = rinv[:, s, :].rearrange("p (b t) -> p b t", b=3)
                dve.tensor_tensor(r3, r3, gates[:, :, hh, :], ALU.mult).then_inc(scale_ready, 1)
                dve.wait_ge(probsT, hh + 1)
                if hh:
                    dve.wait_ge(attended, hh)
                dve.tensor_copy(pT[:, 1, 0:384], bank[3][:, 0:384]).then_inc(bank_free[3], 1)
                dve.tensor_copy(pcT[0:NCMP, s, :], bank[6 + s][0:NCMP, 0:S]).then_inc(bank_free[6 + s], 1)
                if s:
                    dve.wait_ge(attended, hh + 1)
                    b, _ = filled[("o", c)]
                    dve.tensor_tensor(gatt[:, c, :], bank[b][:, 0:S], gatt[:, c, :], ALU.mult).then_inc(bank_free[b], 1)
            dve.wait_ge(conv_sum, 1)
            dve.wait_ge(taps, KC * CONV_W)
            dve.tensor_tensor(cacc, cacc, bank[0][:, 0:S].unsqueeze(1).to_broadcast([P, KC, S]), ALU.subtract)\
               .then_inc(bank_free[0], 1)
            emptied(dve, "cmean")
            dve.tensor_tensor(hf, cacc, cacc, ALU.mult).then_inc(conv_cent, 1)
            dve.wait_ge(conv_var, 1)
            rstd("cvar")
            for c in range(KC):
                dve.scalar_tensor_tensor(hf[:, c, :], cacc[:, c, :], cols[:, CONV_LNG, c:c + 1], std[:], ALU.mult, ALU.mult)\
                   .then_inc(conv_ln, 1)
            operand_rest(O_CONV, lambda c: sq[:, c, :])
            for j in range(KC):
                from_unit(U["pw"] + j) if j < KC - 1 else (lo_to(U["wout"] + RING - 1), dve.wait_ge(unit_done, U["wout"]))
                b, _ = filled[("pw", j)]
                dve.tensor_tensor(cacc[:, j, :], bank[b][:, 0:S], gcon[:, j, :], ALU.mult).then_inc(bank_free[b], 1)
                emptied(dve, ("pw", j))
                if j == 0:
                    dve.wait_ge(conv_act, KC)
                    emptied(dve, ("o", KC - 1))
                    emptied(dve, ("o", KC - 2))
                dve.tensor_tensor(hf[:, j, :], cacc[:, j, :], gatt[:, j, :], ALU.add).then_inc(y_ready, 1)
            operand_rest(O_Y, lambda c: hf[:, c, :])
            residual("wout")
            squares(0, 1)
            normed(1, G_X, hf)
            operand_rest(O_X, lambda c: hf[:, c, :])
            def x_max(h):
                s = h % 2
                dve.wait_ge(xs, h + 1)
                after(dve.tensor_reduce(mx[:, s, 0:TT], bank[s][:, :].rearrange("p (a b) -> p a b", a=TT), AX, ALU.max))
                dve.tensor_scalar(mx[:, s, 0:TT], mx[:, s, 0:TT], -1.0, None, ALU.mult).then_inc(xs_max, 1)

            lo_to(U["xo"] + RING - 1)
            x_max(0)
            for h in range(XH):
                s = h % 2
                if h + 1 < XH:
                    x_max(h + 1)
                emptied(dve, ("xs", h))
                if h >= 2:
                    dve.wait_ge(xs_scaled, h - 1)
                dve.reciprocal(rinv[:, s, 0:TT], sums[:, s, 0:TT]).then_inc(xs_rinv, 1)
                for k in range(2):
                    c = 2 * h + k
                    dve.wait_ge(opnd_hi, KC * O_XO + c + 1)
                    b, _ = filled[("xo_in", c)]
                    dve.tensor_tensor(a_lo[:, c, :], bank[b][:, 0:S], a_hi[:, c, :].bitcast(F32), ALU.subtract)\
                       .then_inc(bank_free[b], 1)
            residual("xo")
            squares(0, 2)
            normed(2, G_FFN, hf)
            operand_rest(O_FFN, lambda c: hf[:, c, :])
            u0, n0 = U["ffn"], base["ffn"]

            def ffn_product(u, par, n):
                dve.wait_ge(unit_done, u + 2)
                dve.wait_ge(bank_free[4 + 2 * par], n)
                dve.tensor_tensor(act2[:, par, :], bank[5 + 2 * par][:, 0:S], act2[:, par, :], ALU.mult)\
                   .then_inc(bank_free[5 + 2 * par], 1)

            def hidden_rest(par, hi_sem, ready, n):
                dve.wait_ge(hi_sem, n)
                dve.tensor_tensor(h_lo[:, par, :], act2[:, par, :], h_hi[:, par, :].bitcast(F32), ALU.subtract)\
                   .then_inc(ready, 1)

            ffn_product(u0, 0, n0[0] + 1)
            hidden_rest(0, hid_hi, hid_ready, 1)
            lo(u0 + RING - 1, (u0 + RING - 1) % RING)
            lo(u0 + RING, (u0 + RING) % RING)
            with dve.Fori(0, 5) as i:
                for k in range(4):
                    u, par = u0 + 2 + 3 * k, (k + 1) % 2
                    lo(i * 12 + (u + 3), (u + 3) % RING)
                    ffn_product(i * 12 + u, par, i * 2 + (n0[2 * par] + 1 + (k + 1) // 2))
                    lo(i * 12 + (u + 4), (u + 4) % RING)
                    hidden_rest(par, hid_hi, hid_ready, i * 4 + (k + 2))
                    lo(i * 12 + (u + 5), (u + 5) % RING)
            f = FC - 1
            u = u0 + 2 + 3 * (f - 1)
            split_done[0] = u + 3
            lo_to(u + RING)
            ffn_product(u, 1, n0[2] + 1 + f // 2)
            lo_to(u + 1 + RING)
            hidden_rest(1, hid_hi, hid_ready, FC)
            lo_to(U["ua"] + RING - 1)
            dve.wait_ge(unit_done, U["ua"])
            for b in range(4):
                dve.tensor_copy(xT[:, 2 * b:2 * b + 2, :].rearrange("p a b -> p (a b)"), bank[b][:, :]).then_inc(bank_free[b], 1)
            for b in range(4):
                emptied(dve, ("ffn", b))
            squares(0, 3)
            normed(3, G_FINAL, xT)
            dve.wait_ge(norm_out, KC * 4)
            squares(0, 4)
            normed(4, G_NORM1, hf)
            operand_rest(O_2, lambda c: hf[:, c, :])
            lo_to(U["va"] + RING)
            dve.wait_ge(unit_done, U["va"] + 1)
            lo_to(U["q2"] + RING - 1)
            dve.wait_ge(const2_in, 64)
            dve.wait_ge(lnv_in, 32)
            for t in range(TT):
                emptied(dve, ("va", t))
                after(dve.bn_stats(stat[:, 8 + 6 * t:14 + 6 * t], va[:, t, :]))
                dve.bn_aggr(stat[:, 2 * t:2 * t + 2], stat[:, 8 + 6 * t:14 + 6 * t]).then_inc(stat_ready, 1)
            lo_to(U["q2"] + RING)
            var = stat[:, 0:4].rearrange("p (t a) -> p t a", a=2)[:, :, 1]
            dve.wait_ge(stat_std, 1)
            after(dve.reciprocal(var, var))
            for t in range(TT):
                after(dve.tensor_scalar(va[:, t, :], va[:, t, :], stat[:, 2 * t:2 * t + 1], stat[:, 2 * t + 1:2 * t + 2],
                                        ALU.subtract, ALU.mult))
                after(dve.tensor_tensor(va[:, t, :], va[:, t, :], lnv[:, 0, :], ALU.mult))
                dve.tensor_tensor(va[:, t, :], va[:, t, :], lnv[:, 1, :], ALU.add).then_inc(ln2, 1)
                lo_to(U["q2"] + RING + 1 + t)
            for n, (name, rows) in enumerate((("q2", q2), ("k2", k2))):
                for j in range(4):
                    lo_to(U[name] + j + RING)
                for t in range(TT):
                    emptied(dve, (name, t))
                    x3 = rows[:, t, :].rearrange("p (a b) -> p a b", b=32)
                    xh = rows[:, t, :].rearrange("p (h a b) -> p h a b", a=2, b=32)
                    ca = tmpA[:, t, :].rearrange("p (h a b) -> p h a b", a=2, b=32)
                    sa = tmpB[:, t, :].rearrange("p (h a b) -> p h a b", a=2, b=32)
                    for k, dst in enumerate((tmpA, tmpB)):
                        ins = dve.tensor_tensor(dst[:, t, :].rearrange("p (a b) -> p a b", b=32), x3,
                                                rope[:, t, k, :].unsqueeze(1).to_broadcast([P, 16, 32]), ALU.mult)
                    after(ins)
                    after(dve.tensor_tensor(xh[:, :, 0, :], ca[:, :, 0, :], sa[:, :, 1, :], ALU.subtract))
                    ins = dve.tensor_tensor(xh[:, :, 1, :], ca[:, :, 1, :], sa[:, :, 0, :], ALU.add)
                    if t == 0:
                        after(ins)
                ins.then_inc(roped, 1)
            for j in range(4):
                lo_to(U["v2"] + j + RING)
            lo_to(U["wout2"] + RING - 1)
            for t in range(TT):
                emptied(dve, ("ua", t))
                dve.wait_ge(mixed, t + 1)
                for g in range(8):
                    g0 = slice(g * 64, (g + 1) * 64)
                    ins = dve.scalar_tensor_tensor(mix[:, 0, t, g0], bank[4 + t][:, g0], bs[:, g:g + 1], ua[:, t, g0],
                                                   ALU.add, ALU.mult)
                ins.then_inc(bank_free[4 + t], 1)
            def bias2(h):
                s = h % 2
                dve.wait_ge(s2, h + 1)
                if h >= 2:
                    dve.wait_ge(p2t, h - 1)
                for t in range(TT):
                    ins = dve.tensor_tensor_reduce(prob2[:, s, t * S:(t + 1) * S], bank[s][:, t * S:(t + 1) * S], lc[:, t, :],
                                                   1.0, -3e38, ALU.add, ALU.max, mx[:, s, t:t + 1])
                ins.then_inc(bank_free[s], 1)
                emptied(dve, ("s2", h))
                dve.tensor_scalar(mx[:, s, 0:TT], mx[:, s, 0:TT], -1.0, None, ALU.mult).then_inc(s2_biased, 1)

            bias2(0)
            for h in range(H2):
                s = h % 2
                if h + 1 < H2:
                    bias2(h + 1)
                dve.wait_ge(s2_exp, h + 1)
                after(dve.reciprocal(rinv[:, s, 0:TT], sums[:, s, 0:TT]))
                dve.wait_ge(o2, h + 1)
                for t in range(TT):
                    ins = dve.tensor_scalar(mix[:, 1, t, h * HD2:(h + 1) * HD2], bank[4 + s][:, t * HD2:(t + 1) * HD2],
                                            rinv[:, s, t:t + 1], None, ALU.mult)
                ins.then_inc(bank_free[4 + s], 1)
            for t in range(TT):
                emptied(dve, ("mixed", t))
            for h in (H2 - 2, H2 - 1):
                emptied(dve, ("o2", h))
            for k in range(2):
                for t in range(TT):
                    after(dve.tensor_tensor_reduce(tmpA[:, 0, :], mix[:, k, t, :], mix[:, k, t, :], 1.0 / 512, 0.0, ALU.mult,
                                                   ALU.add, stat[:, 4 + 2 * k + t:5 + 2 * k + t]))
            dve.tensor_copy(stat[:, 20:21], stat[:, 7:8]).then_inc(stat_ready, 1)
            dve.wait_ge(stat_std, 2)
            after(dve.reciprocal(stat[:, 4:8], stat[:, 4:8]))
            for k in range(2):
                for t in range(TT):
                    dve.tensor_scalar(mix[:, k, t, :], mix[:, k, t, :], stat[:, 4 + 2 * k + t:5 + 2 * k + t], None, ALU.mult)\
                       .then_inc(mix_ready, 1)
            for c in range(KC):
                dve.wait_ge(opnd_hi, KC * O_MIX2 + c + 1)
                b, _ = filled[("mixT", c)]
                dve.scalar_tensor_tensor(a_lo[:, c, :], bank[b][:, 0:S], cols[:, G_OUT2, c:c + 1], a_hi[:, c, :].bitcast(F32),
                                         ALU.mult, ALU.subtract).then_inc(bank_free[b], 1)
            residual("wout2")
            squares(0, 5)
            normed(5, G_NORM2, hf)
            operand_rest(O_PEER, lambda c: hf[:, c, :])
            for j in range(16):
                from_unit(U["wq2"] + j)
            dve.wait_ge(const2_in, 96)
            after(dve.tensor_copy(iota_k[:], iota))

            def top16(x, values, places, spare):
                after(dve.max(values[:, 0:8], x))
                dve.max_index(places[:, 0:8], values[:, 0:8], x)
                after(dve.match_replace(spare, values[:, 0:8], x, -3.4e38))
                after(dve.max(values[:, 8:16], spare))
                after(dve.max_index(places[:, 8:16], values[:, 8:16], spare))

            for t in range(TT):
                for hp in range(2 * PH):
                    emptied(dve, ("sk", t, hp // 4))
                    top16(sc[:, t, hp, :], val[:, t, hp // 2, hp % 2, :], idx[:, t, hp // 2, hp % 2, :], rest[:, 0:NK])
            after(dve.tensor_copy(idxf, idx))
            for t in range(TT):
                after(dve.tensor_tensor(cand[:, t * PH:(t + 1) * PH, :, :], val[:, t, :, 0, :].unsqueeze(3).to_broadcast([P, PH, TOPK, TOPK]),
                                        val[:, t, :, 1, :].unsqueeze(2).to_broadcast([P, PH, TOPK, TOPK]), ALU.add))
            for n in range(TT * PH):
                top16(cand[:, n, :, :].rearrange("p a b -> p (a b)"), cval[:, n, :], cidx[:, n, :], rest)
            dve.tensor_tensor(pick[:, 2, :, :].rearrange("p t (h k) -> p (t h) k", k=TOPK), cval,
                              cval[:, :, 0:1].to_broadcast([P, TT * PH, TOPK]), ALU.subtract).then_inc(c_sub, 1)
            flat = cidx.rearrange("p a b -> p (a b)")
            dve.tensor_scalar(cpart[:, 0, :], flat, 4, None, ALU.logical_shift_right)
            after(dve.tensor_scalar(cpart[:, 1, :], flat, TOPK - 1, None, ALU.bitwise_and))
            after(dve.tensor_copy(cpartf, cpart))
            for t in range(TT):
                for k in range(2):
                    after(dve.tensor_tensor(eq, cpartf[:, k, t * P:(t + 1) * P].unsqueeze(2).to_broadcast([P, P, TOPK]),
                                            iota_k[:, 0:TOPK].unsqueeze(1).to_broadcast([P, P, TOPK]), ALU.is_equal))
                    after(dve.tensor_tensor(prod, eq.rearrange("p (h k) j -> p h k j", h=PH),
                                            idxf[:, t, :, k, :].unsqueeze(2).to_broadcast([P, PH, TOPK, TOPK]), ALU.mult))
                    after(dve.tensor_reduce(pick[:, k, t, :], prod.rearrange("p h k j -> p (h k) j"), AX, ALU.add))
            dve.wait_ge(c_exp, 1)
            w3 = pick[:, 2, :, :].rearrange("p t (h k) -> p (t h) k", k=TOPK)
            after(dve.tensor_reduce(psm, w3, AX, ALU.add))
            after(dve.reciprocal(psm, psm))
            for t in range(TT):
                w3 = pick[:, 2, t, :].rearrange("p (h k) -> p h k", k=TOPK)
                dve.tensor_tensor(w3, w3, psm[:, t * PH:(t + 1) * PH].unsqueeze(2).to_broadcast([P, PH, TOPK]), ALU.mult)\
                   .then_inc(routed, 1)
            for t in range(TT):
                emptied(dve, ("route", t))
            with dve.Fori(0, S // 8) as i:
                for pair in range(4):
                    dve.wait_ge(wall_ps, i * 4 + (pair + 1))
                    for k in range(2):
                        def r(n):
                            return routeT[:, n, bass.ds(i * 8 + (2 * pair + k), 1)]
                        dve.tensor_scalar(hot[:, pair % 2, k, 0, :], iota_k[:], r(0), r(2), ALU.is_equal, ALU.mult)
                        ins = dve.tensor_scalar(hot[:, pair % 2, k, 1, :], iota_k[:], r(1), None, ALU.is_equal)
                    ins.then_inc(hot_ready, 1)
            u0, n0, nw = U["experts"], base["experts"], base["wall"]

            def expert_product(par, tile, n, done):
                dve.wait_ge(bank_free[4 + par], n)
                w = wall[:, bass.ds(tile, 1), :].rearrange("p a t -> p (a t)")
                dve.tensor_tensor(act2[:, par, :], act2[:, par, :], w, ALU.mult).then_inc(prod_e, 1)

            lo_to(u0 + RING - 1)
            for b in (4, 5):
                dve.wait_ge(bank_free[b], n0[b - 4])
            expert_product(0, 0, n0[0] + 1, 0)
            lo(u0 + 3, (u0 + 3) % RING)
            hidden_rest(0, ehid_hi, ehid_ready, 1)
            with dve.Fori(0, NEXP // 2 - 1) as i:
                for k in range(2):
                    u, par = u0 + 1 + 2 * k, (k + 1) % 2
                    lo(i * 4 + (u + 3), (u + 3) % RING)
                    expert_product(par, i * 2 + (1 + k), i + (n0[par] + 1 + (k + 1) // 2), 0)
                    lo(i * 4 + (u + 4), (u + 4) % RING)
                    hidden_rest(par, ehid_hi, ehid_ready, i * 2 + (k + 2))
            n = NEXP - 1
            expert_product(1, n, n0[1] + 1 + n // 2, 0)
            hidden_rest(1, ehid_hi, ehid_ready, NEXP)
            dve.wait_ge(prod_e, NEXP)
            dve.wait_ge(unit_done, UNITS)
            for t in range(TT):
                for half in range(2):
                    after(dve.tensor_copy(fin[:, t, half * 512:(half + 1) * 512], bank[2 * t + half][:, :]))
            dve.tensor_tensor_reduce(fsq[:, 0, :], fin[:, 0, :], fin[:, 0, :], 1.0 / D, 0.0, ALU.mult, ALU.add, sums[:, 0, 0:1])\
               .then_inc(fin_copy, 1)
            dve.tensor_tensor_reduce(fsq[:, 1, :], fin[:, 1, :], fin[:, 1, :], 1.0 / D, 0.0, ALU.mult, ALU.add, sums[:, 0, 1:2])\
               .then_inc(stat_ready, 1)
            dve.wait_ge(stat_std, 3)
            after(dve.reciprocal(sums[:, 0, 0:TT], sums[:, 0, 0:TT]))
            dve.wait_ge(fg_in, 16)
            for t in range(TT):
                dve.scalar_tensor_tensor(fin[:, t, :], fin[:, t, :], sums[:, 0, t:t + 1], fg, ALU.mult, ALU.mult).then_inc(fin_out, 1)


def c_units(w):
    k, n = w.shape
    return w.reshape(KC, P, n // P, P).transpose(2, 1, 0, 3).reshape(n // P, P, D)


def r_units(w):
    return w.reshape(4, 2, P, 512).transpose(0, 2, 1, 3).reshape(4, P, D)


def chunks(v):
    return np.ascontiguousarray(v.reshape(KC, P, -1).transpose(1, 0, 2))


def distance_buckets():
    n = np.arange(S)
    nf = np.maximum(n, 1).astype(np.float32)
    large = 16 + (np.log(nf / np.float32(16)) / np.float32(math.log(8)) * np.float32(16)).astype(np.int32)
    return np.where(n < 16, n, np.minimum(large, 31))


def kernel(**inputs):
    import concourse.bacc as bacc
    from concourse.bass_utils import run_bass_kernel_spmd

    a = {k: np.asarray(v) for k, v in inputs.items()}
    heads = [(2 * gp + g) * R + r for gp in range(2) for r in range(R) for g in range(2)]
    feats = np.concatenate([np.arange(h * HD, (h + 1) * HD) for h in heads])
    w = a["w_in"][0]
    cut = np.cumsum([2 * D, NH * HD] + [G * HD] * 6 + [3 * NH, D, D])
    wu, wq, wkc, wvc, wks, wvs, wkw, wvw, wg, wgc, wga = np.split(w, cut[:-1], axis=1)
    glu = np.stack([wu[:, :D].reshape(D, KC, P), wu[:, D:].reshape(D, KC, P)], axis=2).reshape(D, 2 * D)
    wg = wg.reshape(D, 3, NH)[:, [1, 2, 0]][:, :, heads].reshape(D, 3 * NH)
    gates = np.concatenate([wg, np.zeros((D, P - 3 * NH), np.float32)], axis=1)
    xkv, fin, fout = a["xkv_w"][0], a["ffn_in_w"][0], a["ffn_out_w"][0]
    F = FC * P
    fa, fb, fd = c_units(fin[:, :F]), c_units(fin[:, F:]), fout.reshape(FC, P, D)
    ffn = [fa[0], fb[0]]
    for f in range(1, FC):
        ffn += [fa[f], fb[f], fd[f - 1]]
    ffn.append(fd[FC - 1])
    w2i = a["w_in_2"][0]
    eu = a["expert_u_2"][0].reshape(NEXP, P, KC, P).transpose(0, 3, 2, 1).reshape(NEXP, P, D)
    ev = a["expert_v_2"][0].reshape(NEXP, P, D)
    experts = [eu[0]]
    for n in range(1, NEXP):
        experts += [eu[n], ev[n - 1]]
    experts.append(ev[NEXP - 1])
    stream = np.concatenate([
        c_units(glu), c_units(wq[:, feats]), c_units(wkc), c_units(wvc), c_units(wks), c_units(wkw),
        r_units(np.concatenate([wvs, wvw], axis=1)), c_units(gates), c_units(wgc[:, feats]), c_units(wga[:, feats]),
        c_units(xkv[:, :D]), r_units(xkv[:, D:D + 512]), r_units(xkv[:, D + 512:]),
        c_units(a["conv_pw_w"][0][:, feats]), c_units(a["w_out"][0][feats]), c_units(a["xq_w"][0]), c_units(a["xo_w"][0]),
        np.stack(ffn)] + [r_units(w2i[:, 512 * n:512 * (n + 1)]) for n in range(5)] + [
        c_units(a["w_out_2"][0]), c_units(a["w_query_2"][0]), np.stack(experts)])
    cols = np.stack([chunks(v)[:, :, 0] for v in (
        a["norm_mix_g"][0], a["norm_x_g"][0], a["norm_ffn_g"][0], a["final_norm_g"], a["norm1_g_2"][0], a["norm2_g_2"][0],
        a["conv_dw_b"][0], a["conv_ln_g"][0], a["conv_ln_b"][0],
        np.concatenate([a["out_norm_a_g_2"][0], a["out_norm_b_g_2"][0]]))], axis=1)
    onehot = np.zeros((32, 512), np.float32)
    m = np.arange(S)
    onehot[distance_buckets()[S - 1 - m], m] = 1.0
    q, k = np.arange(S)[:, None], np.arange(S)[None, :]
    seen = (np.abs(q - k) <= 64).astype(int) + ((q - k) % 4 == 0) + ((q - k) % 16 == 0)
    lc = np.where(seen > 0, np.log(np.maximum(seen, 1)), NEG).astype(np.float32).reshape(TT, P, S).transpose(1, 0, 2)
    inv = (1.0 / (np.float32(10000.0) ** (np.arange(0, HD2, 2, dtype=np.float32) / np.float32(HD2)))).astype(np.float32)
    ang = np.arange(S, dtype=np.float32)[:, None] * inv[None, :]
    rope = np.stack([np.cos(ang), np.sin(ang)], axis=1).astype(np.float32).reshape(TT, P, 2, 32).transpose(1, 0, 2, 3)
    host = {
        "stream": stream, "xT": chunks(a["x"][0].T), "memT": chunks(a["mem"][0].T), "cols": cols,
        "dw": chunks(a["conv_dw_w"][0].T), "onehot": onehot, "relb": a["rel_bias"][:, heads],
        "pos": a["cmp_pos"][0].transpose(0, 2, 1), "w1": a["cmp_w1"][0].transpose(0, 2, 1, 3), "w2": a["cmp_w2"][0],
        "ident": np.eye(P, dtype=np.float32), "iota": np.tile(np.arange(P, dtype=np.float32), (P, 1)),
        "lnv": np.stack([a["ln_v_g_2"][0], a["ln_v_b_2"][0]]), "rope": rope,
        "wsT": a["w_spatial_2"][0].transpose(2, 0, 1), "bs": a["b_spatial_2"][0].T, "lc": lc,
        "skT": a["sub_keys_2"][0].transpose(2, 0, 1), "fg": a["final_norm_g_2"][None, :],
    }
    nc = bacc.Bacc("TRN2", target_bir_lowering=False, num_devices=1)
    args, arrays = [], {}
    for name, v in host.items():
        arrays[f"in_{name}"] = np.ascontiguousarray(v)
        args.append(nc.dram_tensor(f"in_{name}", v.shape, F32, kind="ExternalInput").ap())
    out = nc.dram_tensor("out_rows", (S, D), F32, kind="ExternalOutput").ap()
    build(nc, *args, out)
    r = run_bass_kernel_spmd(nc, [arrays], core_ids=[0])
    return r.results[0]["out_rows"].reshape(1, S, D)
```
